# Optimizing a Trainium2 kernel written in Bass

```python
import jax, jax.numpy as jnp
from jax import lax
import numpy as np

D_MODEL = 1024
BATCH = 1
SEQ = 512
DEPTH = 2

CHUNK = 64

D_MIX = D_MODEL
D_CONV = D_MIX // 2
D_POOL = D_MIX - D_CONV
CONV_HEADS = 8
CONV_WIDTH = 31
POOL_WINDOWS = (2, 4, 8, 16)
N_POOL_GROUPS = len(POOL_WINDOWS)
POOL_GROUP = D_POOL // N_POOL_GROUPS
D_IN = 2 * D_CONV + D_POOL

PEER_HEADS = 8
N_KEYS = 128
N_EXPERTS = N_KEYS * N_KEYS
D_KEY = 256
D_HALF = D_KEY // 2
PEER_TOPK = 16
PEER_BLOCK = 128

EPS = 1e-6

kernel_name = "hybrid_conv_pool_peer_encoder"

def rmsnorm(x, g):
    xf = x.astype(jnp.float32)
    y = xf * lax.rsqrt(jnp.mean(xf * xf, axis=-1, keepdims=True) + EPS)
    return (y * g.astype(jnp.float32)).astype(x.dtype)

def modulate(h, shift, scale):
    return h * (1 + scale[:, None, :]) + shift[:, None, :]

def conv_mixer(z_val, z_gate, w_dw, b_dw, ln_g, ln_b):
    u = z_val * jax.nn.sigmoid(z_gate)
    y = lax.conv_general_dilated(
        u, w_dw[:, None, :], window_strides=(1,),
        padding=[(CONV_WIDTH - 1, 0)],
        dimension_numbers=("NWC", "WIO", "NWC"),
        feature_group_count=D_CONV) + b_dw
    yf = y.astype(jnp.float32)
    mu = jnp.mean(yf, axis=-1, keepdims=True)
    var = jnp.mean(jnp.square(yf - mu), axis=-1, keepdims=True)
    yn = (yf - mu) * lax.rsqrt(var + EPS) * ln_g.astype(jnp.float32) + ln_b.astype(jnp.float32)
    return jax.nn.silu(yn).astype(z_val.dtype)

def pool_mixer(z, w_grp, b_grp, scale):
    B, S, _ = z.shape
    zf = z.astype(jnp.float32)
    cs = jnp.cumsum(zf, axis=1)
    t1 = jnp.arange(1, S + 1, dtype=jnp.float32)[None, :, None]
    outs = []
    for g, w in enumerate(POOL_WINDOWS):
        sl = slice(g * POOL_GROUP, (g + 1) * POOL_GROUP)
        csg = cs[:, :, sl]
        lagged = jnp.pad(csg, ((0, 0), (w, 0), (0, 0)))[:, :S]
        cnt = jnp.minimum(t1, float(w))
        outs.append((csg - lagged) / cnt - zf[:, :, sl])
    p = jnp.concatenate(outs, axis=-1).astype(z.dtype).reshape(B, S, N_POOL_GROUPS, POOL_GROUP)
    y = jnp.einsum("bsgc,gcd->bsgd", p, w_grp) + b_grp
    return y.reshape(B, S, D_POOL) * scale

def peer(h, w_q, sub_keys, u_tab, v_tab):
    B, S, D = h.shape
    T = B * S
    hf = h.reshape(T, D)
    q = (hf @ w_q).reshape(T, PEER_HEADS, 2, D_HALF)
    s = jnp.einsum("thpd,hpkd->thpk", q, sub_keys).astype(jnp.float32)
    top_v, top_i = lax.top_k(s, PEER_TOPK)
    comb = (top_v[:, :, 0, :, None] + top_v[:, :, 1, None, :]).reshape(
        T, PEER_HEADS, PEER_TOPK * PEER_TOPK)
    best_v, best_j = lax.top_k(comb, PEER_TOPK)
    i1 = jnp.take_along_axis(top_i[:, :, 0], best_j // PEER_TOPK, axis=-1)
    i2 = jnp.take_along_axis(top_i[:, :, 1], best_j % PEER_TOPK, axis=-1)
    idx = (i1 * N_KEYS + i2).astype(jnp.int32)
    gate = jax.nn.softmax(best_v, axis=-1).astype(h.dtype)
    M = PEER_HEADS * PEER_TOPK
    nb = T // PEER_BLOCK
    xs = hf.reshape(nb, PEER_BLOCK, D)
    ids = idx.reshape(nb, PEER_BLOCK, M)
    gs = gate.reshape(nb, PEER_BLOCK, M)

    def block(args):
        xb, ib, gb = args
        a = jnp.einsum("tmd,td->tm", u_tab[ib], xb)
        wgt = gb * jax.nn.gelu(a, approximate=False)
        return jnp.einsum("tm,tmd->td", wgt, v_tab[ib])

    y = lax.map(block, (xs, ids, gs))
    return y.reshape(B, S, D)

def setup_inputs(seed: int = 0) -> dict:
    key = jax.random.key(seed)
    ks = jax.random.split(key, 24)
    f32 = jnp.float32
    D = D_MODEL

    def nrm(k, shape, scale):
        return jax.random.normal(k, shape, f32) * scale

    return {
        "x": nrm(ks[0], (BATCH, SEQ, D), 1.0),
        "c": nrm(ks[1], (BATCH, D), 1.0),
        "w_ada": nrm(ks[2], (DEPTH, D, 6 * D), 0.5 * D ** -0.5),
        "b_ada": nrm(ks[3], (DEPTH, 6 * D), 0.02),
        "norm1_g": 1.0 + nrm(ks[4], (DEPTH, D), 0.05),
        "norm2_g": 1.0 + nrm(ks[5], (DEPTH, D), 0.05),
        "w_in": nrm(ks[6], (DEPTH, D, D_IN), D ** -0.5),
        "w_out": nrm(ks[7], (DEPTH, D_MIX, D), D_MIX ** -0.5),
        "conv_w": nrm(ks[8], (DEPTH, CONV_WIDTH, D_CONV), CONV_WIDTH ** -0.5),
        "conv_b": nrm(ks[9], (DEPTH, D_CONV), 0.02),
        "conv_ln_g": 1.0 + nrm(ks[10], (DEPTH, D_CONV), 0.05),
        "conv_ln_b": nrm(ks[11], (DEPTH, D_CONV), 0.02),
        "pool_w": nrm(ks[12], (DEPTH, N_POOL_GROUPS, POOL_GROUP, POOL_GROUP), POOL_GROUP ** -0.5),
        "pool_b": nrm(ks[13], (DEPTH, N_POOL_GROUPS, POOL_GROUP), 0.02),
        "pool_scale": 1.0 + nrm(ks[14], (DEPTH, D_POOL), 0.1),
        "peer_wq": nrm(ks[15], (DEPTH, D, PEER_HEADS * D_KEY), D ** -0.5),
        "peer_keys": nrm(ks[16], (DEPTH, PEER_HEADS, 2, N_KEYS, D_HALF), D_HALF ** -0.5),
        "peer_u": nrm(ks[17], (DEPTH, N_EXPERTS, D), D ** -0.5),
        "peer_v": nrm(ks[18], (DEPTH, N_EXPERTS, D), (PEER_HEADS * PEER_TOPK) ** -0.5),
        "final_g": 1.0 + nrm(ks[19], (D,), 0.05),
    }

def reference(x, c, w_ada, b_ada, norm1_g, norm2_g, w_in, w_out, conv_w, conv_b,
              conv_ln_g, conv_ln_b, pool_w, pool_b, pool_scale, peer_wq, peer_keys,
              peer_u, peer_v, final_g):
    cond = jax.nn.silu(c)
    for l in range(DEPTH):
        mod = cond @ w_ada[l] + b_ada[l]
        sh1, sc1, g1, sh2, sc2, g2 = jnp.split(mod, 6, axis=-1)

        h = modulate(rmsnorm(x, norm1_g[l]), sh1, sc1)
        z = h @ w_in[l]
        ya = conv_mixer(z[..., :D_CONV], z[..., D_CONV:2 * D_CONV],
                        conv_w[l], conv_b[l], conv_ln_g[l], conv_ln_b[l])
        yb = pool_mixer(z[..., 2 * D_CONV:], pool_w[l], pool_b[l], pool_scale[l])
        mix = jnp.concatenate([ya, yb], axis=-1) @ w_out[l]
        x = x + g1[:, None, :] * mix

        h = modulate(rmsnorm(x, norm2_g[l]), sh2, sc2)
        x = x + g2[:, None, :] * peer(h, peer_wq[l], peer_keys[l], peer_u[l], peer_v[l])
    return rmsnorm(x, final_g)


_drawn_inputs = setup_inputs


def setup_inputs(seed=0):
    import zlib

    import numpy as np

    out = dict(_drawn_inputs(seed))
    spreads = {}
    factors = {'norm1_g': 3.355,
     'norm2_g': 8.0,
     'conv_b': 8.0,
     'conv_ln_g': 5.498,
     'conv_ln_b': 8.0,
     'pool_b': 8.0,
     'peer_wq': 2.858,
     'peer_keys': 2.828,
     'peer_u': 3.158,
     'peer_v': 2.842}
    for name, (base, spread) in spreads.items():
        noise = np.random.default_rng([zlib.crc32(name.encode()), seed]).standard_normal(out[name].shape)
        drawn = base * np.exp(spread * noise) if base else spread * noise
        out[name] = __import__('jax').numpy.asarray(drawn.astype(out[name].dtype))
    for name, factor in factors.items():
        out[name] = (out[name] * factor).astype(out[name].dtype)
    return out
```

```python
from contextlib import ExitStack

import concourse.bass as bass
from concourse import mybir

ALU = mybir.AluOpType
ACT = mybir.ActivationFunctionType
AX_X = mybir.AxisListType.X
F32 = mybir.dt.float32
F32R = mybir.dt.float32r
BF16 = mybir.dt.bfloat16
U32 = mybir.dt.uint32
I32 = mybir.dt.int32

P = 128
LOWEST = -3.4028234e38

COL_NORM1, COL_NORM2, COL_BADA = 0, 8, 16
COL_CONVB, COL_LNG, COL_LNB, COL_POOLB, COL_POOLS, COL_CONVW = 64, 68, 72, 76, 80, 84


def hybrid_encoder(nc, x_in, c_in, ada_t, win_t, wout_t, wq_t, u_t, v_t, keys_in, poolw_in, small_in,
                   finalg_in, ident_in, out):
    DEPTH, N_ADA = ada_t.shape[0], ada_t.shape[1]
    D = ada_t.shape[3]
    KC = D // P
    T = x_in.shape[2]
    N_WIN, N_WOUT, N_WQ, N_U, N_V = (w.shape[1] for w in (win_t, wout_t, wq_t, u_t, v_t))
    CONV = N_WIN // 3
    TAPS = 31
    WINDOWS = (2, 4, 8, 16)
    HEADS, TOPK = N_WQ // 2, 16
    SEGS = 2 * HEADS
    TT = T // P
    EPS = 1e-6
    RING = 4
    UPAD, ZPAD = TAPS - 1, max(WINDOWS)

    N_ADA_A = 2 * KC
    stages, base = {}, 0
    for name, n in (("ada_a", N_ADA_A), ("win", N_WIN), ("ada_b", N_ADA - N_ADA_A), ("wout", N_WOUT),
                    ("wq", N_WQ), ("u", N_U), ("v", N_V)):
        assert n % RING == 0
        stages[name] = base
        base += n
    ROUNDS = base // RING

    EARLY = N_U // 2
    LATE = N_U - EARLY
    TOK = T // LATE
    GTOK = 64
    GBLOCKS = T // GTOK
    GCH = GTOK // TOK
    PER_BANK = 512 // P

    ga_dram = nc.dram_tensor("ga_scratch", [N_U, P, T], F32, kind="Internal").ap()
    g_dram = nc.dram_tensor("g_scratch", [GBLOCKS, P, N_U, GTOK], F32, kind="Internal").ap()

    ctx = ExitStack()
    with ctx:
        def sb(name, shape, dt=F32):
            return ctx.enter_context(nc.sbuf_tensor(name, shape, dt))

        def sem(name):
            return ctx.enter_context(nc.semaphore(name))

        x = sb("x", [P, KC, T])
        h = sb("h", [P, KC, T])
        h_hi = sb("h_hi", [P, KC, T], F32R)
        h_lo = sb("h_lo", [P, KC, T], F32R)
        ring = sb("ring", [P, RING, KC * P])
        w_hi = sb("w_hi", [P, 2, KC * P], F32R)
        w_lo = sb("w_lo", [P, 2, KC * P], F32R)
        norm_tmp = sb("norm_tmp", [P, 4, T])
        scratch = sb("scratch", [P, 32 * T])
        u_pad = sb("u_pad", [P, CONV, UPAD + T])
        z_pad = sb("z_pad", [P, CONV, ZPAD + T])
        keys = sb("keys", [P, 5 * T])
        small = sb("small", [P, COL_CONVW + CONV * TAPS])
        poolw = sb("poolw", [P, CONV, P])
        ones = sb("ones", [P, P])
        ident = sb("ident", [P, P])
        iota_b = sb("iota_b", [P, P], BF16)
        iota_f = sb("iota_f", [P, 16])
        inv_count = sb("inv_count", [P, 16])
        iota_i = sb("iota_i", [P, P], I32)
        cond = sb("cond", [P, KC])
        finalg = sb("finalg", [P, KC])
        mod = sb("mod", [P, N_ADA])
        coef = sb("coef", [P, 2, KC])

        def part(at, n):
            return scratch[:, at * T:(at + n) * T]

        mix = part(0, 8).rearrange("p (c t) -> p c t", t=T)
        sq = part(8, 8).rearrange("p (c t) -> p c t", t=T)
        conv_y = part(16, 4).rearrange("p (c t) -> p c t", t=T)
        pooled = part(20, 4).rearrange("p (c t) -> p c t", t=T)
        psum_a = part(24, 3)[:, 0:2 * (ZPAD + T)].rearrange("p (c t) -> p c t", t=ZPAD + T)
        conv_odd = part(27, 1)
        sig = part(28, 2).rearrange("p (c t) -> p c t", t=T)
        q_t = part(0, 16).rearrange("p (n t) -> p n t", t=T)
        scores = part(16, 16).rearrange("p (a s k) -> p a s k", a=TT, s=SEGS)
        g_out = part(0, 32).rearrange("p (b i t) -> p b i t", b=2, t=GTOK)
        ga_in = part(0, RING).rearrange("p (s t) -> p s t", t=T)
        g_in = part(RING, RING).rearrange("p (s t) -> p s t", t=T)
        i1_t, i2_t, ghi_t, gmid_t, glo_t = (keys[:, n * T:(n + 1) * T] for n in range(5))
        keys_v = keys[:, 0:SEGS * P].rearrange("p (s k) -> p s k", k=P)
        hf = h[:, :, :].rearrange("p c t -> p (c t)")
        i1_f, i2_f, gate = (hf[:, n * T:(n + 1) * T].rearrange("p (a m) -> p a m", a=TT) for n in range(3))
        rest = hf[:, 3 * T:8 * T]
        vals = rest[:, 0:256].rearrange("p (s k) -> p s k", k=TOPK)
        idx_u = rest[:, 256:512].bitcast(U32).rearrange("p (s k) -> p s k", k=TOPK)
        idx_f = rest[:, 512:768].rearrange("p (s k) -> p s k", k=TOPK)
        best = rest[:, 768:896].rearrange("p (s k) -> p s k", k=TOPK)
        bj = rest[:, 896:1024].bitcast(U32)
        ja_u = rest[:, 1024:1152].bitcast(U32)
        jb_u = rest[:, 1152:1280].bitcast(U32)
        ja_f = rest[:, 1280:1408].rearrange("p (s k) -> p s k", k=TOPK)
        jb_f = rest[:, 1408:1536].rearrange("p (s k) -> p s k", k=TOPK)
        gsum = rest[:, 1536:1536 + TT * HEADS]
        ginv = rest[:, 1600:1600 + TT * HEADS]
        big = u_pad[:, :, :].rearrange("p c t -> p (c t)")[:, 0:SEGS * P]
        big2 = z_pad[:, :, :].rearrange("p c t -> p (c t)")[:, 0:SEGS * P]
        hb = hf.bitcast(BF16)
        hot2 = hb[:, 0:2 * TOK * P].rearrange("p (b j i) -> p b j i", b=2, j=TOK)
        hot1 = hb[:, 2 * TOK * P:8 * TOK * P].rearrange("p (b j q i) -> p b j q i", b=2, j=TOK, q=3)

        bank = ctx.enter_context(nc.psum_tensor("bank", [P, 8, 512], F32))

        tile_landed = [sem(f"tile_landed{s}") for s in range(RING)]
        tile_used = [sem(f"tile_used{s}") for s in range(RING)]
        x_landed, const_landed = sem("x_landed"), sem("const_landed")
        small_landed, poolw_landed, keys_landed = sem("small_landed"), sem("poolw_landed"), sem("keys_landed")
        consts_made, cond_ready = sem("consts_made"), sem("cond_ready")
        x_new = sem("x_new")
        squared, summed, var_ready, root_ready = sem("squared"), sem("summed"), sem("var_ready"), sem("root_ready")
        scaled, h_ready = sem("scaled"), sem("h_ready")
        dve_step, act_step, pool_step = sem("dve_step"), sem("act_step"), sem("pool_step")
        coef_ready = sem("coef_ready")
        sig_ready, u_ready, z_ready = sem("sig_ready"), sem("u_ready"), sem("z_ready")
        pads_zeroed, pooled_ready, pool_product = sem("pads_zeroed"), sem("pooled_ready"), sem("pool_product")
        conv_ready, centered, ln_squared, normed = sem("conv_ready"), sem("centered"), sem("ln_squared"), sem("normed")
        ln_summed = sem("ln_summed")
        mix_a_ready, mix_b_ready = sem("mix_a_ready"), sem("mix_b_ready")
        hi_ready_h, lo_ready_h = sem("hi_ready_h"), sem("lo_ready_h")
        q_ready, score_product, score_ready = sem("q_ready"), sem("score_product"), sem("score_ready")
        split_hi, chunk_done, gelu_done = sem("split_hi"), sem("chunk_done"), sem("gelu_done")
        ga_stored = [sem(f"ga_stored{s}") for s in range(RING)]
        retrieved, exp_done, gate_ready = sem("retrieved"), sem("exp_done"), sem("gate_ready")
        turned = sem("turned")
        hot_ready, gate_product, gate_copied = sem("hot_ready"), sem("gate_product"), sem("gate_copied")
        g_stored = [sem(f"g_stored{b}") for b in range(2)]
        ga_landed = [sem(f"ga_landed{s}") for s in range(RING)]
        g_landed = [sem(f"g_landed{s}") for s in range(RING)]
        w_step, w_ready = sem("w_step"), sem("w_ready")
        out_ready, out_stored = sem("out_ready"), sem("out_stored")

        ROOTS = 3
        CHUNKS = N_U + N_V

        def wait_landed(eng, l, stage, first, n):
            at = stages[stage] + n
            eng.wait_ge(tile_landed[at % RING], 16 * ROUNDS * l + 16 * first + 16 * (at // RING) + 16)

        def wait_used(eng, l, stage, first, n):
            at = stages[stage] + n
            eng.wait_ge(tile_used[at % RING], ROUNDS * l + first + (at // RING) + 2)

        def settle(eng):
            eng.nop(nofuse=True)

        block = ctx.enter_context(nc.Block())

        @block.sync
        def _(sp):
            sp.dma_start(x[:, :, :], x_in).then_inc(x_landed, 16)
            sp.dma_start(cond[:, :], c_in).then_inc(const_landed, 16)
            sp.dma_start(finalg[:, :], finalg_in).then_inc(const_landed, 16)
            sp.dma_start(ident[:, :], ident_in).then_inc(const_landed, 16)

            def load_tile(l, src, stage, first, n, i):
                at = stages[stage] + n
                sp.wait_ge(tile_used[at % RING], ROUNDS * l + first + at // RING + 1)
                sp.dma_start(ring[:, at % RING, :], src[l, i]).then_inc(tile_landed[at % RING], 16)

            def stream(l, src, stage, skip, count):
                with sp.Fori(0, count // RING) as r:
                    for s in range(RING):
                        load_tile(l, src, stage, r, s, RING * r + (skip + s))

            with sp.Fori(0, DEPTH) as l:
                stream(l, ada_t, "ada_a", 0, N_ADA_A)
                stream(l, win_t, "win", 0, N_WIN)
                stream(l, ada_t, "ada_b", N_ADA_A, N_ADA - N_ADA_A)
                stream(l, wout_t, "wout", 0, N_WOUT)
                stream(l, wq_t, "wq", 0, N_WQ)
                stream(l, u_t, "u", 0, N_U)
                for s in range(RING):
                    load_tile(l, v_t, "v", 0, s, s)
                for s in range(RING):
                    sp.wait_ge(ga_stored[s], 16 * (N_U // RING) * l + 16 * (N_U // RING) + 16)
                for b in range(2):
                    sp.wait_ge(g_stored[b], 16 * (GBLOCKS // 2) * l + 16 * (GBLOCKS // 2) + 16)
                settle(sp)

                def load_back(r, s):
                    c = RING * r + s
                    sp.wait_ge(w_ready, N_V * l + RING * r + s + 1)
                    sp.dma_start(ga_in[:, s, :], ga_dram[c]).then_inc(ga_landed[s], 16)
                    sp.dma_start(g_in[:, s, :].rearrange("p (b t) -> p b t", t=GTOK),
                                 g_dram[:, :, c, :].rearrange("b p t -> p b t")).then_inc(g_landed[s], 16)

                with sp.Fori(0, N_V // RING - 1) as r:
                    for s in range(RING):
                        load_back(r, s)
                        load_tile(l, v_t, "v", r, RING + s, RING * r + (RING + s))
                for s in range(RING):
                    load_back(N_V // RING - 1, s)

            for k in range(KC):
                sp.wait_ge(out_ready, k + 1)
                sp.dma_start(out[:, k, :], h[:, k, :]).then_inc(out_stored, 16)
            sp.wait_ge(out_stored, 16 * KC)

        @block.tensor
        def _(pe):
            for s in range(RING):
                pe.nop().then_inc(tile_used[s], 1)
            pe.nop().then_inc(chunk_done, 2)
            pe.nop().then_inc(gate_product, 2)
            pe.wait_ge(const_landed, 48)
            pe.wait_ge(consts_made, 2)

            def sum_squares(n_norm):
                for k in range(KC):
                    pe.wait_ge(squared, KC * n_norm + (k + 1))
                    mm = pe.matmul(bank[:, 0, :], ones[:, :], sq[:, k, :], start=(k == 0), stop=(k == KC - 1))
                mm.then_inc(summed, 1)

            def product(to, s, rhs, sem_done):
                for k in range(KC):
                    mm = pe.matmul(to, ring[:, s, k * P:(k + 1) * P], rhs(k), start=(k == 0), stop=(k == KC - 1))
                mm.then_inc(sem_done, 1)

            def ada(l, stage, skip, count):
                with pe.Fori(0, count // RING) as r:
                    for s in range(RING):
                        wait_landed(pe, l, stage, r, s)
                        product(bank[:, 1, bass.ds(RING * r + (skip + s), 1)], s, lambda k: cond[:, k:k + 1], tile_used[s])

            pe.wait_ge(cond_ready, 1)
            with pe.Fori(0, DEPTH) as l:
                pe.wait_ge(x_new, 2 * KC * l + 1)
                settle(pe)
                ada(l, "ada_a", 0, N_ADA_A)
                sum_squares(2 * l)
                for n in range(N_WIN):
                    wait_landed(pe, l, "win", 0, n)
                    if n == 0:
                        pe.wait_ge(h_ready, 2 * KC * l + KC)
                    if n >= 6:
                        pe.wait_ge(u_ready if n % 2 else sig_ready, CONV * l + ((n - 6) // 2 + 1))
                    product(bank[:, 2 + n % 6, :], n % RING, lambda k: h[:, k, :], tile_used[n % RING])
                pe.wait_ge(coef_ready, 2 * l + 1)
                settle(pe)
                ada(l, "ada_b", N_ADA_A, N_ADA - N_ADA_A)
                pe.wait_ge(poolw_landed, 16 * l + 16)
                for g in range(CONV):
                    pe.wait_ge(pooled_ready, CONV * l + (g + 1))
                    pe.matmul(bank[:, 4 + g, :], poolw[:, g, :], pooled[:, g, :], start=True, stop=True)\
                      .then_inc(pool_product, 1)
                for j in range(CONV):
                    pe.wait_ge(conv_ready, CONV * l + (j + 1))
                    mm = pe.matmul(bank[:, 0, :], ones[:, :], conv_y[:, j, :], start=(j == 0), stop=(j == CONV - 1))
                mm.then_inc(ln_summed, 1)
                pe.wait_ge(centered, CONV * l + CONV)
                for j in range(CONV):
                    pe.wait_ge(ln_squared, CONV * l + (j + 1))
                    mm = pe.matmul(bank[:, 0, :], ones[:, :], sq[:, j, :], start=(j == 0), stop=(j == CONV - 1))
                mm.then_inc(ln_summed, 1)
                pe.wait_ge(mix_b_ready, CONV * l + CONV)
                pe.wait_ge(mix_a_ready, CONV * l + CONV)
                for n in range(N_WOUT):
                    wait_landed(pe, l, "wout", 0, n)
                    if n >= 6:
                        pe.wait_ge(x_new, 2 * KC * l + (n - 6 + 2))
                    product(bank[:, 2 + n % 6, :], n % RING, lambda k: mix[:, k, :], tile_used[n % RING])
                sum_squares(2 * l + 1)
                for n in range(N_WQ):
                    wait_landed(pe, l, "wq", 0, n)
                    if n == 0:
                        pe.wait_ge(h_ready, 2 * KC * l + 2 * KC)
                    if n >= 6:
                        pe.wait_ge(q_ready, N_WQ * l + (n - 6 + 1))
                    product(bank[:, 2 + n % 6, :], n % RING, lambda k: h[:, k, :], tile_used[n % RING])
                pe.wait_ge(q_ready, N_WQ * l + N_WQ)
                pe.wait_ge(keys_landed, 16 * l + 16)
                for a in range(TT):
                    if a >= 2:
                        pe.wait_ge(score_ready, 4 * TT * l + 4 * (a - 1))
                    for s in range(SEGS):
                        mm = pe.matmul(bank[:, 4 * (a % 2) + s // 4, (s % 4) * P:(s % 4 + 1) * P],
                                       q_t[:, s, a * P:(a + 1) * P], keys_v[:, s, :], start=True, stop=True)
                        if s % 4 == 3:
                            mm.then_inc(score_product, 1)

                def up_chunk(l, r, n):
                    b = n % 2
                    pe.wait_ge(gelu_done, N_U * l + RING * r + n + 1)
                    pe.wait_ge(split_hi, CHUNKS * l + RING * r + n + 1)
                    for k in range(KC):
                        for part_h in (h_hi, h_lo):
                            pe.matmul(bank[:, b, :], w_hi[:, b, k * P:(k + 1) * P], part_h[:, k, :],
                                      start=(k == 0 and part_h is h_hi), stop=False)
                    wait_used(pe, l, "u", r, n)
                    for k in range(KC):
                        mm = pe.matmul(bank[:, b, :], w_lo[:, b, k * P:(k + 1) * P], h_hi[:, k, :],
                                       start=False, stop=(k == KC - 1))
                    mm.then_inc(chunk_done, 1)

                pe.wait_ge(lo_ready_h, KC * l + KC)
                pe.wait_ge(score_ready, 4 * TT * l + 4 * TT)
                settle(pe)
                with pe.Fori(0, EARLY // RING) as r:
                    for s in range(RING):
                        up_chunk(l, r, s)
                pe.wait_ge(gate_ready, l + 1)
                for n, src in enumerate((i1_f, i2_f, gate)):
                    for a in range(TT):
                        mm = pe.transpose(bank[:, 2 + n, a * P:(a + 1) * P], src[:, a, :], ident[:, :])
                mm.then_inc(turned, 1)

                with pe.Fori(0, LATE // RING) as r:
                    for s in range(RING):
                        up_chunk(l, r + EARLY // RING, s)
                        b = s % 2
                        pe.wait_ge(hot_ready, LATE * l + RING * r + s + 1)
                        pe.wait_ge(gate_copied, LATE * l + RING * r + s + 1)
                        for j in range(TOK):
                            to = bank[:, 2 + 2 * b + j // PER_BANK, (j % PER_BANK) * P:(j % PER_BANK + 1) * P]
                            for q in range(3):
                                mm = pe.matmul(to, hot2[:, b, j, :], hot1[:, b, j, q, :], start=(q == 0), stop=(q == 2))
                        mm.then_inc(gate_product, 1)

                def down_chunk(l, r, n, first=False, last=False):
                    b = n % 2
                    pe.wait_ge(split_hi, CHUNKS * l + RING * r + (N_U + n + 1))
                    pe.wait_ge(w_ready, N_V * l + RING * r + (n + 1 + RING))
                    for k in range(KC):
                        for part_w in (h_hi, h_lo):
                            pe.matmul(bank[:, k, :], w_hi[:, b, k * P:(k + 1) * P], part_w[:, b, :],
                                      start=(first and part_w is h_hi), stop=False)
                    wait_used(pe, l, "v", r, n)
                    for k in range(KC):
                        mm = pe.matmul(bank[:, k, :], w_lo[:, b, k * P:(k + 1) * P], h_hi[:, b, :],
                                       start=False, stop=last)
                    mm.then_inc(chunk_done, 1)

                pe.wait_ge(gelu_done, N_U * l + N_U + 2)
                pe.wait_ge(gate_copied, LATE * l + LATE + 2)
                for s in range(RING):
                    down_chunk(l, 0, s, first=(s == 0))
                with pe.Fori(1, N_V // RING - 1) as r:
                    for s in range(RING):
                        down_chunk(l, r, s)
                for s in range(RING):
                    down_chunk(l, N_V // RING - 1, s, last=(s == RING - 1))
            sum_squares(2 * DEPTH)

        @block.scalar
        def _(act):
            def copy(to, of):
                return act.activation(to, of, ACT.Copy)

            act.nop().then_inc(gelu_done, 2)
            act.nop().then_inc(gate_copied, 2)
            for s in range(RING):
                act.nop().then_inc(ga_stored[s], 16)
            for b in range(2):
                act.nop().then_inc(g_stored[b], 16)
            act.wait_ge(const_landed, 48)
            act.activation(cond[:, :], cond[:, :], ACT.Silu).then_inc(cond_ready, 1)

            def squares(n_norm, x_count):
                act.wait_ge(x_new, x_count)
                for k in range(KC):
                    act.activation(sq[:, k, :], x[:, k, :], ACT.Square).then_inc(squared, 1)

            def root(n_root):
                act.wait_ge(var_ready, n_root + 1)
                act.activation(norm_tmp[:, 1, :], norm_tmp[:, 0, :], ACT.Sqrt).then_inc(root_ready, 1)

            with act.Fori(0, DEPTH) as l:
                squares(2 * l, 2 * KC * l + 1)
                act.dma_start(small[:, :], small_in[l]).then_inc(small_landed, 16)
                act.dma_start(poolw[:, :, :], poolw_in[l]).then_inc(poolw_landed, 16)
                act.dma_start(keys_v, keys_in[l]).then_inc(keys_landed, 16)
                root(ROOTS * l)

                def shift(n_norm, col):
                    for k in range(KC):
                        act.wait_ge(scaled, KC * n_norm + (k + 1))
                        act.activation(h[:, k, :], h[:, k, :], ACT.Identity, bias=mod[:, col + k:col + k + 1])\
                           .then_inc(h_ready, 1)

                act.wait_ge(coef_ready, 2 * l + 1)
                shift(2 * l, 0)
                for j in range(CONV):
                    wait_used(act, l, "win", 0, 2 * j)
                    if j >= 2:
                        act.wait_ge(u_ready, CONV * l + (j - 1))
                    act.activation(sig[:, j % 2, :], bank[:, 2 + (2 * j) % 6, :], ACT.Sigmoid).then_inc(sig_ready, 1)
                act.wait_ge(pads_zeroed, l + 1)
                for g in range(CONV):
                    n = 2 * CONV + g
                    wait_used(act, l, "win", 0, n)
                    copy(z_pad[:, g, ZPAD:], bank[:, 2 + n % 6, :]).then_inc(z_ready, 1)
                for j in range(CONV):
                    act.wait_ge(centered, CONV * l + (j + 1))
                    act.activation(sq[:, j, :], conv_y[:, j, :], ACT.Square).then_inc(ln_squared, 1)
                root(ROOTS * l + 1)
                for j in range(CONV):
                    act.wait_ge(normed, CONV * l + (j + 1))
                    act.activation(mix[:, j, :], conv_y[:, j, :], ACT.Silu, bias=small[:, COL_LNB + j:COL_LNB + j + 1],
                                   scale=small[:, COL_LNG + j:COL_LNG + j + 1]).then_inc(mix_a_ready, 1)
                squares(2 * l + 1, 2 * KC * l + (KC + 1))
                root(ROOTS * l + 2)
                shift(2 * l + 1, 3 * KC)
                for k in range(KC):
                    act.wait_ge(h_ready, 2 * KC * l + (KC + k + 1))
                    copy(h_hi[:, k, :], h[:, k, :]).then_inc(hi_ready_h, 1)

                def hi(l, r, n):
                    wait_landed(act, l, "u", r, n)
                    act.wait_ge(chunk_done, CHUNKS * l + RING * r + (n + 1))
                    copy(w_hi[:, n % 2, :], ring[:, n % RING, :]).then_inc(split_hi, 1)

                for n in range(N_WQ):
                    wait_used(act, l, "wq", 0, n)
                    copy(q_t[:, n, :], bank[:, 2 + n % 6, :]).then_inc(q_ready, 1)
                hi(l, 0, 0)
                for a in range(TT):
                    for b in range(4):
                        act.wait_ge(score_product, 4 * TT * l + (4 * a + b + 1))
                        copy(scores[:, a, 4 * b:4 * b + 4, :],
                             bank[:, 4 * (a % 2) + b, :].rearrange("p (s k) -> p s k", k=P)).then_inc(score_ready, 1)

                def gelu(l, r, n):
                    act.wait_ge(chunk_done, CHUNKS * l + RING * r + (n + 3))
                    act.wait_ge(ga_stored[n % RING], 16 * (N_U // RING) * l + 16 * r + 16)
                    act.activation(norm_tmp[:, n, :], bank[:, n % 2, :], ACT.Gelu).then_inc(gelu_done, 1)
                    act.wait_ge(gelu_done, N_U * l + RING * r + (n + 3))
                    act.dma_start(ga_dram[RING * r + n], norm_tmp[:, n, :]).then_inc(ga_stored[n], 16)

                with act.Fori(0, EARLY // RING) as r:
                    for s in range(RING):
                        hi(l, r, s + 1)
                        gelu(l, r, s)
                act.wait_ge(retrieved, TT * l + TT)
                act.activation(gate[:, :, :], gate[:, :, :], ACT.Exp).then_inc(exp_done, 1)
                with act.Fori(0, GBLOCKS // 2) as pair:
                    for b in range(2):
                        for n in range(GCH):
                            r = 2 * GCH // RING * pair + (EARLY + GCH * b + n) // RING
                            s = (GCH * b + n) % RING
                            hi(l, r, s + 1)
                            gelu(l, r, s)
                            act.wait_ge(gate_product, LATE * l + 2 * GCH * pair + (GCH * b + n + 3))
                            if n == 0:
                                act.wait_ge(g_stored[b], 16 * (GBLOCKS // 2) * l + 16 * pair + 16)
                            for half in range(TOK // PER_BANK):
                                t0 = n * TOK + half * PER_BANK
                                ins = copy(g_out[:, b, :, t0:t0 + PER_BANK],
                                           bank[:, 2 + 2 * (s % 2) + half, :].rearrange("p (t i) -> p i t", i=P))
                            ins.then_inc(gate_copied, 1)
                        act.wait_ge(gate_copied, LATE * l + 2 * GCH * pair + (GCH * b + GCH + 2))
                        act.dma_start(g_dram[2 * pair + b], g_out[:, b, :, :]).then_inc(g_stored[b], 16)
                with act.Fori(0, N_V // RING - 1) as r:
                    for s in range(RING):
                        hi(l, r + N_U // RING, s + 1)
                for s in range(RING - 1):
                    hi(l, (N_U + N_V) // RING - 1, s + 1)
            squares(2 * DEPTH, 2 * KC * DEPTH + 1)
            root(ROOTS * DEPTH)

        @block.gpsimd
        def _(pool):
            pool.memset(ones[:, :], 1.0).then_inc(consts_made, 1)
            pool.iota(iota_i[:, :], [[1, P]], base=0, channel_multiplier=0).then_inc(pool_step, 1)
            pool.wait_ge(pool_step, 1)
            pool.tensor_copy(iota_f[:, :], iota_i[:, 0:16]).then_inc(pool_step, 1)
            pool.tensor_copy(iota_b[:, :], iota_i[:, :]).then_inc(consts_made, 1)
            steps = [2]
            STEPS = 18

            with pool.Fori(0, DEPTH) as l:
                pool.wait_ge(x_new, 2 * KC * l + 1)
                settle(pool)
                pool.memset(u_pad[:, :, 0:UPAD], 0.0)
                pool.memset(z_pad[:, :, 0:ZPAD], 0.0)
                pool.memset(psum_a[:, :, 0:ZPAD], 0.0).then_inc(pads_zeroed, 1)
                pool.wait_ge(pads_zeroed, l + 1)

                def step(ins):
                    steps[0] += 1
                    ins.then_inc(pool_step, 1)
                    pool.wait_ge(pool_step, STEPS * l + steps[0])
                    settle(pool)

                for g, w in enumerate(WINDOWS):
                    pool.wait_ge(z_ready, CONV * l + (g + 1))
                    src, width = z_pad[:, g, :], 1
                    flip = 0
                    while width < w:
                        dst = psum_a[:, flip, :]
                        step(pool.tensor_tensor(dst[:, ZPAD:], src[:, ZPAD:], src[:, ZPAD - width:ZPAD + T - width], ALU.add))
                        src, width, flip = dst, 2 * width, 1 - flip
                    other = psum_a[:, flip, :]
                    step(pool.tensor_scalar(other[:, ZPAD:], src[:, ZPAD:], 1.0 / w, 0.0, ALU.mult, ALU.add))
                    step(pool.tensor_tensor(other[:, ZPAD:ZPAD + w], src[:, ZPAD:ZPAD + w], inv_count[:, 0:w], ALU.mult))
                    pool.tensor_tensor(pooled[:, g, :], other[:, ZPAD:], z_pad[:, g, ZPAD:], ALU.subtract)\
                        .then_inc(pooled_ready, 1)
                    pool.wait_ge(pooled_ready, CONV * l + (g + 1))
                settle(pool)
                assert steps[0] == STEPS + 2, steps

                with pool.Fori(0, CHUNKS // RING) as r:
                    for s in range(RING):
                        pool.wait_ge(split_hi, CHUNKS * l + RING * r + (s + 1))
                        pool.tensor_tensor(w_lo[:, s % 2, :], ring[:, s, :], w_hi[:, s % 2, :].bitcast(F32), ALU.subtract)\
                            .then_inc(tile_used[s], 1)

        @block.vector
        def _(dve):
            steps = [0]
            STEPS = 3 * 5 + 2 + CONV * TAPS + TT * (5 * (SEGS + HEADS) + 12) + 10

            dve.nop().then_inc(w_ready, RING)
            dve.wait_ge(consts_made, 2)
            dve.tensor_scalar(inv_count[:, :], iota_f[:, :], 1.0, None, ALU.add).then_inc(dve_step, 1)
            dve.wait_ge(dve_step, 1)
            dve.reciprocal(inv_count[:, :], inv_count[:, :]).then_inc(dve_step, 1)
            dve.wait_ge(dve_step, 2)
            dve.wait_ge(x_landed, 16)
            dve.nop().then_inc(x_new, 1)
            FIRST = 2

            def count(ins):
                steps[0] += 1
                ins.then_inc(dve_step, 1)

            def rstd(l, n_root, to_var):
                v, r0, r, t = (norm_tmp[:, n, :] for n in range(4))
                to_var(v).then_inc(var_ready, 1)
                dve.wait_ge(root_ready, n_root + 1)

                def link(ins):
                    count(ins)
                    dve.wait_ge(dve_step, STEPS * l + (FIRST + steps[0]))

                link(dve.reciprocal(r, r0))
                link(dve.tensor_tensor(t, r, r, ALU.mult))
                link(dve.tensor_tensor(t, t, v, ALU.mult))
                link(dve.tensor_scalar(t, t, -0.5, 1.5, ALU.mult, ALU.add))
                link(dve.tensor_tensor(r, r, t, ALU.mult))
                return r

            def norm(l, n_norm, n_root, coefs, done):
                dve.wait_ge(summed, n_norm + 1)
                r = rstd(l, n_root, lambda v: dve.tensor_scalar(v, bank[:, 0, :], 1.0 / D, EPS, ALU.mult, ALU.add))
                for k in range(KC):
                    dve.scalar_tensor_tensor(h[:, k, :], x[:, k, :], coefs[:, k:k + 1], r, ALU.mult, ALU.mult)\
                       .then_inc(done, 1)

            with dve.Fori(0, DEPTH) as l:
                def link(ins):
                    count(ins)
                    dve.wait_ge(dve_step, STEPS * l + (FIRST + steps[0]))

                def modulation(stage, a, b, gain, scale_col, which):
                    last = N_ADA_A if stage == "ada_a" else N_ADA - N_ADA_A
                    wait_used(dve, l, stage, 0, last - 1)
                    link(dve.tensor_tensor(mod[:, a:b], bank[:, 1, a:b], small[:, COL_BADA + a:COL_BADA + b], ALU.add))
                    dve.scalar_tensor_tensor(coef[:, which, :], mod[:, scale_col:scale_col + KC], 1.0,
                                             small[:, gain:gain + KC], ALU.add, ALU.mult).then_inc(coef_ready, 1)
                    dve.wait_ge(coef_ready, 2 * l + (which + 1))

                dve.wait_ge(small_landed, 16 * l + 16)
                modulation("ada_a", 0, N_ADA_A, COL_NORM1, KC, 0)
                norm(l, 2 * l, ROOTS * l, coef[:, 0, :], scaled)

                dve.wait_ge(pads_zeroed, l + 1)
                for j in range(CONV):
                    dve.wait_ge(sig_ready, CONV * l + (j + 1))
                    wait_used(dve, l, "win", 0, 2 * j + 1)
                    dve.tensor_tensor(u_pad[:, j, UPAD:], bank[:, 2 + (2 * j + 1) % 6, :], sig[:, j % 2, :], ALU.mult)\
                       .then_inc(u_ready, 1)
                    dve.wait_ge(u_ready, CONV * l + (j + 1))
                    for k in range(TAPS):
                        w = small[:, COL_CONVW + j * TAPS + k:COL_CONVW + j * TAPS + k + 1]
                        acc = conv_y[:, j, :] if k % 2 == 0 else conv_odd
                        src = u_pad[:, j, k:k + T]
                        if k >= 2:
                            dve.wait_ge(dve_step, STEPS * l + (FIRST + steps[0] - 1))
                        if k == 0:
                            count(dve.tensor_scalar(acc, src, w, small[:, COL_CONVB + j:COL_CONVB + j + 1], ALU.mult, ALU.add))
                        elif k == 1:
                            count(dve.tensor_scalar(acc, src, w, None, ALU.mult))
                        else:
                            count(dve.scalar_tensor_tensor(acc, src, w, acc, ALU.mult, ALU.add))
                    dve.wait_ge(dve_step, STEPS * l + (FIRST + steps[0]))
                    dve.tensor_tensor(conv_y[:, j, :], conv_y[:, j, :], conv_odd, ALU.add).then_inc(conv_ready, 1)
                    dve.wait_ge(conv_ready, CONV * l + (j + 1))

                for g in range(CONV):
                    dve.wait_ge(pool_product, CONV * l + (g + 1))
                    dve.tensor_scalar(mix[:, CONV + g, :], bank[:, 4 + g, :], small[:, COL_POOLB + g:COL_POOLB + g + 1],
                                      small[:, COL_POOLS + g:COL_POOLS + g + 1], ALU.add, ALU.mult).then_inc(mix_b_ready, 1)

                modulation("ada_b", N_ADA_A, N_ADA, COL_NORM2, 4 * KC, 1)

                dve.wait_ge(ln_summed, 2 * l + 1)
                for j in range(CONV):
                    dve.scalar_tensor_tensor(conv_y[:, j, :], bank[:, 0, :], -1.0 / (CONV * P), conv_y[:, j, :],
                                             ALU.mult, ALU.add).then_inc(centered, 1)
                dve.wait_ge(ln_summed, 2 * l + 2)
                r = rstd(l, ROOTS * l + 1,
                         lambda v: dve.tensor_scalar(v, bank[:, 0, :], 1.0 / (CONV * P), EPS, ALU.mult, ALU.add))
                for j in range(CONV):
                    dve.tensor_tensor(conv_y[:, j, :], conv_y[:, j, :], r, ALU.mult).then_inc(normed, 1)

                for n in range(N_WOUT):
                    wait_used(dve, l, "wout", 0, n)
                    dve.scalar_tensor_tensor(x[:, n, :], bank[:, 2 + n % 6, :], mod[:, 2 * KC + n:2 * KC + n + 1],
                                             x[:, n, :], ALU.mult, ALU.add).then_inc(x_new, 1)
                norm(l, 2 * l + 1, ROOTS * l + 2, coef[:, 1, :], scaled)
                for k in range(KC):
                    dve.wait_ge(hi_ready_h, KC * l + (k + 1))
                    dve.tensor_tensor(h_lo[:, k, :], h[:, k, :], h_hi[:, k, :].bitcast(F32), ALU.subtract)\
                       .then_inc(lo_ready_h, 1)

                dve.wait_ge(q_ready, N_WQ * l + N_WQ)
                dve.wait_ge(lo_ready_h, KC * l + KC)

                def every(n, make):
                    for s in range(n):
                        count(make(s))
                    dve.wait_ge(dve_step, STEPS * l + (FIRST + steps[0]))
                    settle(dve)

                def top16(n, values, spare, v_of, i_of):
                    every(n, lambda s: dve.max(v_of(s)[:, 0:8], values(s)))
                    every(n, lambda s: dve.max_index(i_of(s)[:, 0:8], v_of(s)[:, 0:8], values(s)))
                    every(n, lambda s: dve.match_replace(spare(s), v_of(s)[:, 0:8], values(s), LOWEST))
                    every(n, lambda s: dve.max(v_of(s)[:, 8:16], spare(s)))
                    every(n, lambda s: dve.max_index(i_of(s)[:, 8:16], v_of(s)[:, 8:16], spare(s)))

                big_s = big.rearrange("p (s k) -> p s k", k=P)
                big_c = big.rearrange("p (s k) -> p s k", k=TOPK * TOPK)
                big_4 = big.rearrange("p (s i j) -> p s i j", i=TOPK, j=TOPK)
                eq_4 = big2.rearrange("p (s i j) -> p s i j", i=TOPK, j=TOPK)
                shape4 = [P, HEADS, TOPK, TOPK]
                v2 = vals.rearrange("p (h e) k -> p h e k", e=2)
                i2 = idx_f.rearrange("p (h e) k -> p h e k", e=2)
                bj_v = bj.rearrange("p (s k) -> p s k", k=TOPK)
                for a in range(TT):
                    dve.wait_ge(score_ready, 4 * TT * l + 4 * (a + 1))
                    settle(dve)
                    sc_a = scores[:, a, :, :]
                    sc_c = sc_a.rearrange("p s k -> p (s k)").rearrange("p (s k) -> p s k", k=TOPK * TOPK)
                    top16(SEGS, lambda s: sc_a[:, s, :], lambda s: big_s[:, s, :], lambda s: vals[:, s, :],
                          lambda s: idx_u[:, s, :])
                    link(dve.tensor_tensor(big_4, v2[:, :, 0, :].unsqueeze(3).to_broadcast(shape4),
                                           v2[:, :, 1, :].unsqueeze(2).to_broadcast(shape4), ALU.add))
                    settle(dve)
                    top16(HEADS, lambda s: big_c[:, s, :], lambda s: sc_c[:, s, :], lambda s: best[:, s, :],
                          lambda s: bj_v[:, s, :])
                    count(dve.tensor_scalar(ja_u, bj, 4, None, ALU.logical_shift_right))
                    link(dve.tensor_scalar(jb_u, bj, TOPK - 1, None, ALU.bitwise_and))
                    count(dve.tensor_copy(idx_f[:, :, :], idx_u[:, :, :]))
                    count(dve.tensor_copy(ja_f.rearrange("p s k -> p (s k)"), ja_u))
                    link(dve.tensor_copy(jb_f.rearrange("p s k -> p (s k)"), jb_u))
                    for half, (jf, to) in enumerate(((ja_f, i1_f), (jb_f, i2_f))):
                        link(dve.tensor_tensor(eq_4, jf.unsqueeze(3).to_broadcast(shape4),
                                               iota_f[:, :].unsqueeze(1).unsqueeze(1).to_broadcast(shape4), ALU.is_equal))
                        link(dve.tensor_tensor(eq_4, eq_4, i2[:, :, half, :].unsqueeze(2).to_broadcast(shape4), ALU.mult))
                        link(dve.tensor_reduce(to[:, a, :].rearrange("p (h k) -> p h k", k=TOPK), eq_4, AX_X, ALU.add))
                    dve.tensor_tensor(gate[:, a, :].rearrange("p (h k) -> p h k", k=TOPK), best[:, :, :],
                                      best[:, :, 0:1].to_broadcast([P, HEADS, TOPK]), ALU.subtract).then_inc(retrieved, 1)
                    dve.wait_ge(retrieved, TT * l + (a + 1))
                dve.wait_ge(exp_done, l + 1)
                gate_v = gate.rearrange("p a (h k) -> p (a h) k", k=TOPK)
                link(dve.tensor_reduce(gsum, gate_v, AX_X, ALU.add))
                link(dve.reciprocal(ginv, gsum))
                dve.tensor_tensor(gate_v, gate_v, ginv.unsqueeze(2).to_broadcast([P, TT * HEADS, TOPK]), ALU.mult)\
                   .then_inc(gate_ready, 1)
                dve.wait_ge(turned, l + 1)
                count(dve.tensor_copy(i1_t, bank[:, 2, :]))
                count(dve.tensor_copy(i2_t, bank[:, 3, :]))
                gb = hf[:, 3 * T:4 * T].bitcast(BF16)[:, 0:T]
                link(dve.tensor_copy(gb, bank[:, 4, :]))
                link(dve.tensor_copy(ghi_t, gb))
                link(dve.tensor_tensor(glo_t, bank[:, 4, :], ghi_t, ALU.subtract))
                link(dve.tensor_copy(gb, glo_t))
                link(dve.tensor_copy(gmid_t, gb))
                link(dve.tensor_tensor(glo_t, glo_t, gmid_t, ALU.subtract))
                settle(dve)

                with dve.Fori(0, LATE // RING) as r:
                    for s in range(RING):
                        b = s % 2
                        dve.wait_ge(gate_product, LATE * l + RING * r + (s + 1))
                        for j in range(TOK):
                            t = RING * TOK * r + (s * TOK + j)
                            col = bass.ds(t, 1)
                            dve.tensor_scalar(hot2[:, b, j, :], iota_b[:, :], i2_t[:, col], None, ALU.is_equal)
                            for q, g_part in enumerate((ghi_t, gmid_t, glo_t)):
                                ins = dve.tensor_scalar(hot1[:, b, j, q, :], iota_b[:, :], i1_t[:, col], g_part[:, col],
                                                        ALU.is_equal, ALU.mult)
                        ins.then_inc(hot_ready, 1)

                with dve.Fori(0, N_V // RING) as r:
                    for s in range(RING):
                        b = s % 2
                        dve.wait_ge(ga_landed[s], 16 * (N_V // RING) * l + 16 * r + 16)
                        dve.wait_ge(g_landed[s], 16 * (N_V // RING) * l + 16 * r + 16)
                        dve.tensor_tensor(ga_in[:, s, :], ga_in[:, s, :], g_in[:, s, :], ALU.mult).then_inc(w_step, 1)
                        dve.wait_ge(w_step, 2 * N_V * l + 2 * RING * r + (2 * s + 1))
                        dve.wait_ge(chunk_done, CHUNKS * l + RING * r + (N_U + s + 1))
                        dve.tensor_copy(h_hi[:, b, :], ga_in[:, s, :]).then_inc(w_step, 1)
                        dve.wait_ge(w_step, 2 * N_V * l + 2 * RING * r + (2 * s + 2))
                        dve.tensor_tensor(h_lo[:, b, :], ga_in[:, s, :], h_hi[:, b, :].bitcast(F32), ALU.subtract)\
                           .then_inc(w_ready, 1)
                dve.wait_ge(chunk_done, CHUNKS * l + CHUNKS + 2)
                for k in range(KC):
                    dve.scalar_tensor_tensor(x[:, k, :], bank[:, k, :], mod[:, 5 * KC + k:5 * KC + k + 1],
                                             x[:, k, :], ALU.mult, ALU.add).then_inc(x_new, 1)
                assert steps[0] == STEPS, steps
            steps[0] = 0
            norm(DEPTH, 2 * DEPTH, ROOTS * DEPTH, finalg, out_ready)


def kernel(**inputs):
    import numpy as np
    import concourse.bacc as bacc
    from concourse.bass_utils import run_bass_kernel_spmd

    L = inputs["w_ada"].shape[0]
    D = inputs["w_ada"].shape[1]
    KC = D // P

    def tiles(w):
        n = w.shape[2] // P
        return np.ascontiguousarray(w.reshape(L, KC, P, n, P).transpose(0, 3, 2, 1, 4).reshape(L, n, P, KC * P))

    def columns(v):
        return v.reshape(L, -1, P).transpose(0, 2, 1)

    a = {k: np.asarray(v) for k, v in inputs.items()}
    conv = a["conv_w"].shape[2] // P
    order = [b for j in range(conv) for b in (conv + j, j)] + list(range(2 * conv, 3 * conv))
    experts = a["peer_u"].shape[1] // P
    taps = a["conv_w"].transpose(0, 2, 1).reshape(L, conv, P, -1).transpose(0, 2, 1, 3).reshape(L, P, -1)
    arrays = {
        "x_in": a["x"][0].T.reshape(KC, P, -1).transpose(1, 0, 2),
        "c_in": a["c"][0].reshape(KC, P).T,
        "ada_t": tiles(a["w_ada"]),
        "win_t": tiles(a["w_in"])[:, order],
        "wout_t": tiles(a["w_out"]),
        "wq_t": tiles(a["peer_wq"]),
        "u_t": a["peer_u"].reshape(L, experts, P, KC, P).transpose(0, 1, 4, 3, 2).reshape(L, experts, P, D),
        "v_t": a["peer_v"].reshape(L, experts, P, D),
        "keys_in": a["peer_keys"].transpose(0, 4, 1, 2, 3).reshape(L, P, -1, P),
        "poolw_in": a["pool_w"].transpose(0, 2, 1, 3),
        "small_in": np.concatenate([
            columns(a["norm1_g"]), columns(a["norm2_g"]), columns(a["b_ada"]), columns(a["conv_b"]),
            columns(a["conv_ln_g"]), columns(a["conv_ln_b"]), columns(a["pool_b"].reshape(L, -1)),
            columns(a["pool_scale"]), taps], axis=2),
        "finalg_in": a["final_g"].reshape(KC, P).T,
        "ident_in": np.eye(P, dtype=np.float32),
    }
    nc = bacc.Bacc("TRN2", target_bir_lowering=False, num_devices=1)
    args = {}
    for name, v in arrays.items():
        arrays[name] = v = np.ascontiguousarray(v)
        args[name] = nc.dram_tensor(name, v.shape, mybir.dt.from_np(v.dtype), kind="ExternalInput").ap()
    seq = a["x"].shape[1]
    out = nc.dram_tensor("out", [P, KC, seq], F32, kind="ExternalOutput").ap()
    hybrid_encoder(nc, out=out, **args)
    got = run_bass_kernel_spmd(nc, [arrays], core_ids=[0]).results[0]["out"]
    return np.ascontiguousarray(got.transpose(2, 1, 0).reshape(1, seq, D))
```

```python
from contextlib import ExitStack

import concourse.bass as bass
from concourse import mybir

ALU = mybir.AluOpType
ACT = mybir.ActivationFunctionType
AX_X = mybir.AxisListType.X
F32 = mybir.dt.float32
F32R = mybir.dt.float32r
F16 = mybir.dt.float16
U32 = mybir.dt.uint32
I32 = mybir.dt.int32

P = 128
LOWEST = -3.4028234e38
GATE_UP = 16384.0

COL_NORM1, COL_NORM2, COL_BADA = 0, 8, 16
COL_CONVB, COL_LNG, COL_LNB, COL_POOLB, COL_POOLS, COL_CONVW = 64, 68, 72, 76, 80, 84


def hybrid_encoder(nc, x_in, c_in, ada_t, win_t, wout_t, wq_t, u_t, v_t, keys_in, poolw_in, small_in,
                   finalg_in, ident_in, out):
    DEPTH, N_ADA = ada_t.shape[0], ada_t.shape[1]
    D = ada_t.shape[3]
    KC = D // P
    LAST = DEPTH - 1
    T = x_in.shape[2]
    N_WIN, N_WOUT, N_WQ, N_U, N_V = (w.shape[1] for w in (win_t, wout_t, wq_t, u_t, v_t))
    CONV = N_WIN // 3
    TAPS = 31
    WINDOWS = (2, 4, 8, 16)
    HEADS, TOPK = N_WQ // 2, 16
    SEGS = 2 * HEADS
    TT = T // P
    EPS = 1e-6
    RING = 4
    UPAD, ZPAD = TAPS - 1, max(WINDOWS)

    stages, base = {}, 0
    for name, n in (("win", N_WIN), ("wout", N_WOUT), ("wq", N_WQ), ("u", N_U), ("v", N_V)):
        assert n % RING == 0
        stages[name] = base
        base += n
    CHUNKS = base
    ROUNDS = CHUNKS // RING
    ADA_STEP = 2
    ADA_ROUNDS = N_ADA // ADA_STEP

    RETRIEVING = 9 * N_U // 32
    EARLY, LATE = RETRIEVING + 2 * RING, N_U // 2
    TOK = T // LATE
    GTOK = 64
    GBLOCKS = T // GTOK
    GCH = GTOK // TOK
    PER_BANK = 512 // P

    ga_dram = nc.dram_tensor("ga_scratch", [N_U, P, T], F32, kind="Internal").ap()
    g_dram = nc.dram_tensor("g_scratch", [GBLOCKS, P, N_U, GTOK], F32, kind="Internal").ap()

    ctx = ExitStack()
    with ctx:
        def sb(name, shape, dt=F32):
            return ctx.enter_context(nc.sbuf_tensor(name, shape, dt))

        def sem(name):
            return ctx.enter_context(nc.semaphore(name))

        x = sb("x", [P, KC, T])
        h = sb("h", [P, KC, T])
        h_hi = sb("h_hi", [P, KC, T], F32R)
        h_lo = sb("h_lo", [P, KC, T], F32R)
        ring = sb("ring", [P, RING, KC * P])
        w_hi = sb("w_hi", [P, 2, KC * P], F32R)
        w_lo = sb("w_lo", [P, 2, KC * P], F32R)
        v_hi = sb("v_hi", [P, 2, T], F32R)
        v_lo = sb("v_lo", [P, 2, T], F32R)
        norm_tmp = sb("norm_tmp", [P, 4, T])
        scratch = sb("scratch", [P, 32 * T])
        u_pad = sb("u_pad", [P, CONV, UPAD + T])
        z_pad = sb("z_pad", [P, CONV, ZPAD + T])
        keys = sb("keys", [P, SEGS * P])
        small = sb("small", [P, COL_CONVW + CONV * TAPS])
        ones = sb("ones", [P, P])
        ident = sb("ident", [P, P])
        iota_b = sb("iota_b", [P, P], F16)
        iota_f = sb("iota_f", [P, 16])
        inv_count = sb("inv_count", [P, 16])
        cond = sb("cond", [P, D])
        finalg = sb("finalg", [P, KC])
        mod_sum = sb("mod_sum", [P, N_ADA])
        mod = sb("mod", [P, N_ADA])
        coef = sb("coef", [P, 2, KC])

        def part(at, n):
            return scratch[:, at * T:(at + n) * T]

        mix = part(0, 8).rearrange("p (c t) -> p c t", t=T)
        sq = part(8, 8).rearrange("p (c t) -> p c t", t=T)
        conv_y = part(16, 4).rearrange("p (c t) -> p c t", t=T)
        pooled = part(20, 4).rearrange("p (c t) -> p c t", t=T)
        psum_a = part(24, 3)[:, 0:2 * (ZPAD + T)].rearrange("p (c t) -> p c t", t=ZPAD + T)
        conv_odd = part(27, 1)
        sig = part(28, 2).rearrange("p (c t) -> p c t", t=T)
        poolw = part(30, 1).rearrange("p (g d) -> p g d", d=P)
        iota_i = part(31, 1)[:, 0:P].bitcast(I32)
        ada = part(16, 8).rearrange("p (s c) -> p s c", c=D)
        q_t = part(0, 16).rearrange("p (n t) -> p n t", t=T)
        scores = part(16, 16).rearrange("p (a s k) -> p a s k", a=TT, s=SEGS)
        g_out = part(0, 32).rearrange("p (b i t) -> p b i t", b=2, t=GTOK)
        ga_in = part(0, RING).rearrange("p (s t) -> p s t", t=T)
        g_in = part(RING, RING).rearrange("p (s t) -> p s t", t=T)
        i1_t, i2_t, ghi_t, glo_t = (keys[:, n * T:(n + 1) * T] for n in range(4))
        keys_v = keys[:, :].rearrange("p (s k) -> p s k", k=P)
        hf = h[:, :, :].rearrange("p c t -> p (c t)")
        i1_f, i2_f, gate = (hf[:, n * T:(n + 1) * T].rearrange("p (a m) -> p a m", a=TT) for n in range(3))
        rest = hf[:, 3 * T:8 * T]
        vals = rest[:, 0:256].rearrange("p (s k) -> p s k", k=TOPK)
        idx_u = rest[:, 256:512].bitcast(U32).rearrange("p (s k) -> p s k", k=TOPK)
        idx_f = rest[:, 512:768].rearrange("p (s k) -> p s k", k=TOPK)
        best = rest[:, 768:896].rearrange("p (s k) -> p s k", k=TOPK)
        bj = rest[:, 896:1024].bitcast(U32)
        ja_u = rest[:, 1024:1152].bitcast(U32)
        jb_u = rest[:, 1152:1280].bitcast(U32)
        ja_f = rest[:, 1280:1408].rearrange("p (s k) -> p s k", k=TOPK)
        jb_f = rest[:, 1408:1536].rearrange("p (s k) -> p s k", k=TOPK)
        gsum = rest[:, 1536:1536 + TT * HEADS]
        ginv = rest[:, 1600:1600 + TT * HEADS]
        big = u_pad[:, :, :].rearrange("p c t -> p (c t)")[:, 0:SEGS * P]
        big2 = z_pad[:, :, :].rearrange("p c t -> p (c t)")[:, 0:SEGS * P]
        hb = hf.bitcast(F16)
        hot2 = hb[:, 0:2 * TOK * P].rearrange("p (b j i) -> p b j i", b=2, j=TOK)
        hot1 = hb[:, 2 * TOK * P:6 * TOK * P].rearrange("p (b j q i) -> p b j q i", b=2, j=TOK, q=2)

        bank = ctx.enter_context(nc.psum_tensor("bank", [P, 8, 512], F32))

        tile_landed = [sem(f"tile_landed{s}") for s in range(RING)]
        tile_used = [sem(f"tile_used{s}") for s in range(RING)]
        x_landed, const_landed, cond_landed = sem("x_landed"), sem("const_landed"), sem("cond_landed")
        small_landed, poolw_landed, keys_landed = sem("small_landed"), sem("poolw_landed"), sem("keys_landed")
        consts_made, cond_ready = sem("consts_made"), sem("cond_ready")
        x_new = sem("x_new")
        squared, summed, var_ready, root_ready = sem("squared"), sem("summed"), sem("var_ready"), sem("root_ready")
        scaled, h_ready = sem("scaled"), sem("h_ready")
        dve_step, act_step, pool_step = sem("dve_step"), sem("act_step"), sem("pool_step")
        coef_ready = sem("coef_ready")
        ada_landed = [sem(f"ada_landed{s}") for s in range(RING)]
        ada_used = [sem(f"ada_used{s}") for s in range(RING)]
        sig_ready, u_ready, z_ready = sem("sig_ready"), sem("u_ready"), sem("z_ready")
        pads_zeroed, pooled_ready, pool_product = sem("pads_zeroed"), sem("pooled_ready"), sem("pool_product")
        conv_ready, centered, ln_squared, normed = sem("conv_ready"), sem("centered"), sem("ln_squared"), sem("normed")
        ln_summed = sem("ln_summed")
        mix_a_ready, mix_b_ready = sem("mix_a_ready"), sem("mix_b_ready")
        hi_ready_h, lo_ready_h = sem("hi_ready_h"), sem("lo_ready_h")
        q_ready, score_product, score_ready = sem("q_ready"), sem("score_product"), sem("score_ready")
        split_hi, chunk_done, gelu_done = sem("split_hi"), sem("chunk_done"), sem("gelu_done")
        ga_stored = [sem(f"ga_stored{s}") for s in range(RING)]
        retrieved, exp_done, gate_ready = sem("retrieved"), sem("exp_done"), sem("gate_ready")
        turned = sem("turned")
        hot_ready, gate_product, gate_copied = sem("hot_ready"), sem("gate_product"), sem("gate_copied")
        g_stored = [sem(f"g_stored{b}") for b in range(2)]
        ga_landed = [sem(f"ga_landed{s}") for s in range(RING)]
        g_landed = [sem(f"g_landed{s}") for s in range(RING)]
        w_step, w_ready = sem("w_step"), sem("w_ready")
        out_ready, out_stored = sem("out_ready"), sem("out_stored")

        ROOTS = 3

        def wait_landed(eng, l, first, n):
            eng.wait_ge(tile_landed[n % RING], 16 * ROUNDS * l + 16 * first + 16 * (n // RING) + 16)

        def wait_hi(eng, l, first, n):
            eng.wait_ge(split_hi, CHUNKS * l + RING * first + (n + 1))

        def wait_lo(eng, l, first, n):
            eng.wait_ge(tile_used[n % RING], ROUNDS * l + first + (n // RING) + 2)

        def wait_product(eng, l, first, n):
            eng.wait_ge(chunk_done, CHUNKS * l + RING * first + (n + 3))

        def wait_ada(eng, sems, base, l, s, r):
            eng.wait_ge(sems[s], base * (N_ADA // RING) + base * ADA_ROUNDS * l + base * r + base)

        def settle(eng):
            eng.nop(nofuse=True)

        block = ctx.enter_context(nc.Block())

        @block.sync
        def _(sp):
            sp.dma_start(x[:, :, :], x_in).then_inc(x_landed, 16)
            sp.dma_start(cond[:, :], c_in.to_broadcast([P, D])).then_inc(cond_landed, 16)
            sp.dma_start(finalg[:, :], finalg_in).then_inc(const_landed, 16)
            sp.dma_start(ident[:, :], ident_in).then_inc(const_landed, 16)
            with sp.Fori(0, N_ADA // RING) as r:
                for s in range(RING):
                    sp.wait_ge(ada_used[s], r + 1)
                    sp.dma_start(ada[:, s, :], ada_t[0, RING * r + s]).then_inc(ada_landed[s], 16)

            def load_tile(l, src, i, first, n):
                sp.wait_ge(tile_used[n % RING], ROUNDS * l + first + (n // RING + 1))
                sp.dma_start(ring[:, n % RING, :], src[l, i]).then_inc(tile_landed[n % RING], 16)

            with sp.Fori(0, DEPTH) as l:
                for stage, src in (("win", win_t), ("wout", wout_t), ("wq", wq_t), ("u", u_t)):
                    with sp.Fori(0, src.shape[1] // RING) as r:
                        for s in range(RING):
                            load_tile(l, src, RING * r + s, r, stages[stage] + s)

                def load_back(first, n):
                    c, slot = RING * first + n, n % RING
                    sp.wait_ge(w_ready, N_V * l + RING * first + (n + 1))
                    sp.dma_start(ga_in[:, slot, :], ga_dram[c]).then_inc(ga_landed[slot], 16)
                    sp.dma_start(g_in[:, slot, :].rearrange("p (b t) -> p b t", t=GTOK),
                                 g_dram[:, :, c, :].rearrange("b p t -> p b t")).then_inc(g_landed[slot], 16)

                load_tile(l, v_t, 0, 0, stages["v"])
                for b in range(2):
                    sp.wait_ge(g_stored[b], 16 * (GBLOCKS // 2) * l + 16 * (GBLOCKS // 2) + 16)
                for s in range(RING):
                    sp.wait_ge(ga_stored[s], 16 * (N_U // RING) * l + 16 * (N_U // RING - 2) + 16)
                for n in range(RING - 1):
                    load_back(0, n)
                for s in range(1, RING):
                    load_tile(l, v_t, s, 0, stages["v"] + s)
                for s in range(RING):
                    sp.wait_ge(ga_stored[s], 16 * (N_U // RING) * l + 16 * (N_U // RING) + 16)
                settle(sp)

                def rounds(start, end, with_ada):
                    with sp.Fori(start, end) as r:
                        for s in range(ADA_STEP if with_ada else 0):
                            wait_ada(sp, ada_used, 1, l, s, r)
                            sp.dma_start(ada[:, s, :], ada_t[(l + 1) % DEPTH, ADA_STEP * r + s]).then_inc(ada_landed[s], 16)
                        for s in range(RING):
                            load_back(r, s + RING - 1)
                            load_tile(l, v_t, RING * r + (RING + s), r, stages["v"] + RING + s)

                with sp.If(l < LAST):
                    rounds(0, ADA_ROUNDS, True)
                with sp.Else():
                    rounds(0, ADA_ROUNDS, False)
                rounds(ADA_ROUNDS, N_V // RING - 1, False)
                load_back(N_V // RING - 1, RING - 1)

            for k in range(KC):
                sp.wait_ge(out_ready, k + 1)
                sp.dma_start(out[:, k, :], h[:, k, :]).then_inc(out_stored, 16)
            sp.wait_ge(out_stored, 16 * KC)

        @block.tensor
        def _(pe):
            for s in range(RING):
                pe.nop().then_inc(tile_used[s], 1)
            pe.nop().then_inc(chunk_done, 2)
            pe.nop().then_inc(gate_product, 2)
            pe.wait_ge(const_landed, 32)
            pe.wait_ge(consts_made, 2)

            def sum_squares(n_norm):
                for k in range(KC):
                    pe.wait_ge(squared, KC * n_norm + (k + 1))
                    mm = pe.matmul(bank[:, 0, :], ones[:, :], sq[:, k, :], start=(k == 0), stop=(k == KC - 1))
                mm.then_inc(summed, 1)

            def product(l, first, n, to):
                b = n % 2
                wait_hi(pe, l, first, n)
                for k in range(KC):
                    for part_h in (h_hi, h_lo):
                        pe.matmul(to, w_hi[:, b, k * P:(k + 1) * P], part_h[:, k, :],
                                  start=(k == 0 and part_h is h_hi), stop=False)
                wait_lo(pe, l, first, n)
                for k in range(KC):
                    mm = pe.matmul(to, w_lo[:, b, k * P:(k + 1) * P], h_hi[:, k, :], start=False, stop=(k == KC - 1))
                mm.then_inc(chunk_done, 1)

            with pe.Fori(0, DEPTH) as l:
                sum_squares(2 * l)
                pe.wait_ge(lo_ready_h, 3 * KC * l + KC)
                for n in range(N_WIN):
                    if n >= 6:
                        pe.wait_ge(u_ready if n % 2 else sig_ready, CONV * l + ((n - 6) // 2 + 1))
                    product(l, 0, stages["win"] + n, bank[:, 2 + n % 6, :])
                pe.wait_ge(poolw_landed, 16 * l + 16)
                for g in range(CONV):
                    pe.wait_ge(pooled_ready, CONV * l + (g + 1))
                    pe.matmul(bank[:, 4 + g, :], poolw[:, g, :], pooled[:, g, :], start=True, stop=True)\
                      .then_inc(pool_product, 1)
                for j in range(CONV):
                    pe.wait_ge(conv_ready, CONV * l + (j + 1))
                    mm = pe.matmul(bank[:, 0, :], ones[:, :], conv_y[:, j, :], start=(j == 0), stop=(j == CONV - 1))
                mm.then_inc(ln_summed, 1)
                pe.wait_ge(centered, CONV * l + CONV)
                for j in range(CONV):
                    pe.wait_ge(ln_squared, CONV * l + (j + 1))
                    mm = pe.matmul(bank[:, 0, :], ones[:, :], sq[:, j, :], start=(j == 0), stop=(j == CONV - 1))
                mm.then_inc(ln_summed, 1)
                pe.wait_ge(lo_ready_h, 3 * KC * l + 2 * KC)
                for n in range(N_WOUT):
                    if n >= 6:
                        pe.wait_ge(x_new, 2 * KC * l + (n - 6 + 2))
                    product(l, 0, stages["wout"] + n, bank[:, 2 + n % 6, :])
                sum_squares(2 * l + 1)
                pe.wait_ge(lo_ready_h, 3 * KC * l + 3 * KC)
                for n in range(N_WQ):
                    if n >= 6:
                        pe.wait_ge(q_ready, N_WQ * l + (n - 6 + 1))
                    product(l, 0, stages["wq"] + n, bank[:, 2 + n % 6, :])
                pe.wait_ge(q_ready, N_WQ * l + N_WQ)
                pe.wait_ge(keys_landed, 16 * l + 16)
                for a in range(TT):
                    if a >= 2:
                        pe.wait_ge(score_ready, 4 * TT * l + 4 * (a - 1))
                    for s in range(SEGS):
                        mm = pe.matmul(bank[:, 4 * (a % 2) + s // 4, (s % 4) * P:(s % 4 + 1) * P],
                                       q_t[:, s, a * P:(a + 1) * P], keys_v[:, s, :], start=True, stop=True)
                        if s % 4 == 3:
                            mm.then_inc(score_product, 1)

                def up_chunk(r, s):
                    pe.wait_ge(gelu_done, N_U * l + RING * r + s + 1)
                    product(l, r, stages["u"] + s, bank[:, s % 2, :])

                pe.wait_ge(score_ready, 4 * TT * l + 4 * TT)
                settle(pe)
                with pe.Fori(0, RETRIEVING // RING + 1) as r:
                    for s in range(RING):
                        up_chunk(r, s)
                pe.wait_ge(gate_ready, l + 1)
                for n, src in enumerate((i1_f, i2_f, gate)):
                    for a in range(TT):
                        mm = pe.transpose(bank[:, 2 + n, a * P:(a + 1) * P], src[:, a, :], ident[:, :])
                mm.then_inc(turned, 1)
                for s in range(RING):
                    up_chunk(RETRIEVING // RING + 1, s)

                with pe.Fori(0, LATE // RING) as r:
                    for s in range(RING):
                        up_chunk(r + EARLY // RING, s)
                        b = s % 2
                        pe.wait_ge(hot_ready, LATE * l + RING * r + s + 1)
                        pe.wait_ge(gate_copied, LATE * l + RING * r + s + 1)
                        for j in range(TOK):
                            to = bank[:, 2 + 2 * b + j // PER_BANK, (j % PER_BANK) * P:(j % PER_BANK + 1) * P]
                            for q in range(2):
                                mm = pe.matmul(to, hot2[:, b, j, :], hot1[:, b, j, q, :], start=(q == 0), stop=(q == 1))
                        mm.then_inc(gate_product, 1)

                with pe.Fori((EARLY + LATE) // RING, N_U // RING) as r:
                    for s in range(RING):
                        up_chunk(r, s)

                def down_chunk(r, s, first=False, last=False):
                    b = s % 2
                    wait_hi(pe, l, r, stages["v"] + s)
                    pe.wait_ge(w_ready, N_V * l + RING * r + (s + 1 + RING))
                    for k in list(range(2, KC)) + [0, 1]:
                        if first and k == 0:
                            pe.wait_ge(gelu_done, N_U * l + N_U + 2)
                        for part_w in (v_hi, v_lo):
                            pe.matmul(bank[:, k, :], w_hi[:, b, k * P:(k + 1) * P], part_w[:, b, :],
                                      start=(first and part_w is v_hi), stop=False)
                    wait_lo(pe, l, r, stages["v"] + s)
                    for k in range(KC):
                        mm = pe.matmul(bank[:, k, :], w_lo[:, b, k * P:(k + 1) * P], v_hi[:, b, :],
                                       start=False, stop=last)
                    mm.then_inc(chunk_done, 1)

                pe.wait_ge(gate_copied, LATE * l + LATE + 2)
                for s in range(RING):
                    down_chunk(0, s, first=(s == 0))
                with pe.Fori(1, N_V // RING - 1) as r:
                    for s in range(RING):
                        down_chunk(r, s)
                for s in range(RING):
                    down_chunk(N_V // RING - 1, s, last=(s == RING - 1))
            sum_squares(2 * DEPTH)

        @block.scalar
        def _(act):
            def copy(to, of):
                return act.activation(to, of, ACT.Copy)

            act.nop().then_inc(gelu_done, 2)
            act.nop().then_inc(gate_copied, 2)
            for s in range(RING):
                act.nop().then_inc(ga_stored[s], 16)
            for b in range(2):
                act.nop().then_inc(g_stored[b], 16)
            act.wait_ge(cond_landed, 16)
            act.activation(cond[:, :], cond[:, :], ACT.Silu).then_inc(cond_ready, 1)

            def squares(n_norm, x_count):
                act.wait_ge(x_new, x_count)
                for k in range(KC):
                    act.activation(sq[:, k, :], x[:, k, :], ACT.Square).then_inc(squared, 1)

            def root(n_root):
                act.wait_ge(var_ready, n_root + 1)
                act.activation(norm_tmp[:, 1, :], norm_tmp[:, 0, :], ACT.Sqrt).then_inc(root_ready, 1)

            with act.Fori(0, DEPTH) as l:
                def hi(first, n):
                    wait_landed(act, l, first, n)
                    wait_product(act, l, first, n - 2)
                    copy(w_hi[:, n % 2, :], ring[:, n % RING, :]).then_inc(split_hi, 1)

                squares(2 * l, 2 * KC * l + 1)
                act.dma_start(small[:, :], small_in[l]).then_inc(small_landed, 16)
                act.dma_start(poolw[:, :, :], poolw_in[l]).then_inc(poolw_landed, 16)
                act.dma_start(keys_v, keys_in[l]).then_inc(keys_landed, 16)
                root(ROOTS * l)
                hi(0, 0)
                hi(0, 1)

                def shift_hi(n_norm, col):
                    for k in range(KC):
                        act.wait_ge(scaled, KC * n_norm + (k + 1))
                        act.activation(h_hi[:, k, :], h[:, k, :], ACT.Identity, bias=mod[:, col + k:col + k + 1])\
                           .then_inc(hi_ready_h, 1)

                act.wait_ge(coef_ready, 2 * l + 2)
                shift_hi(2 * l, 0)
                act.wait_ge(pads_zeroed, l + 1)
                for n in range(N_WIN):
                    wait_product(act, l, 0, n)
                    if n < 2 * CONV and n % 2 == 0:
                        j = n // 2
                        if j >= 2:
                            act.wait_ge(u_ready, CONV * l + (j - 1))
                        act.activation(sig[:, j % 2, :], bank[:, 2 + n % 6, :], ACT.Sigmoid).then_inc(sig_ready, 1)
                    if n >= 2 * CONV:
                        copy(z_pad[:, n - 2 * CONV, ZPAD:], bank[:, 2 + n % 6, :]).then_inc(z_ready, 1)
                    hi(0, n + 2)
                for g in range(CONV):
                    act.wait_ge(mix_b_ready, CONV * l + (g + 1))
                    copy(h_hi[:, CONV + g, :], mix[:, CONV + g, :]).then_inc(hi_ready_h, 1)
                for j in range(CONV):
                    act.wait_ge(centered, CONV * l + (j + 1))
                    act.activation(sq[:, j, :], conv_y[:, j, :], ACT.Square).then_inc(ln_squared, 1)
                root(ROOTS * l + 1)
                for j in range(CONV):
                    act.wait_ge(normed, CONV * l + (j + 1))
                    act.activation(mix[:, j, :], conv_y[:, j, :], ACT.Silu, bias=small[:, COL_LNB + j:COL_LNB + j + 1],
                                   scale=small[:, COL_LNG + j:COL_LNG + j + 1]).then_inc(mix_a_ready, 1)
                for j in range(CONV):
                    act.wait_ge(mix_a_ready, CONV * l + (j + 1))
                    copy(h_hi[:, j, :], mix[:, j, :]).then_inc(hi_ready_h, 1)
                for n in range(N_WOUT):
                    hi(0, stages["wout"] + n + 2)
                squares(2 * l + 1, 2 * KC * l + (KC + 1))
                root(ROOTS * l + 2)
                shift_hi(2 * l + 1, 3 * KC)
                for n in range(N_WQ):
                    hi(0, stages["wq"] + n + 2)
                    copy(q_t[:, n, :], bank[:, 2 + n % 6, :]).then_inc(q_ready, 1)
                for a in range(TT):
                    for b in range(4):
                        act.wait_ge(score_product, 4 * TT * l + (4 * a + b + 1))
                        copy(scores[:, a, 4 * b:4 * b + 4, :],
                             bank[:, 4 * (a % 2) + b, :].rearrange("p (s k) -> p s k", k=P)).then_inc(score_ready, 1)

                def gelu(r, s):
                    act.wait_ge(ga_stored[s], 16 * (N_U // RING) * l + 16 * r + 16)
                    act.activation(norm_tmp[:, s, :], bank[:, s % 2, :], ACT.Gelu).then_inc(gelu_done, 1)
                    act.wait_ge(gelu_done, N_U * l + RING * r + (s + 3))
                    act.dma_start(ga_dram[RING * r + s], norm_tmp[:, s, :]).then_inc(ga_stored[s], 16)

                act.preload_act_table(ACT.Gelu)
                with act.Fori(0, RETRIEVING // RING) as r:
                    for s in range(RING):
                        hi(r, stages["u"] + s + 2)
                        gelu(r, s)
                act.wait_ge(retrieved, TT * l + TT)
                act.activation(gate[:, :, :], gate[:, :, :], ACT.Exp).then_inc(exp_done, 1)
                act.preload_act_table(ACT.Gelu)
                for r in range(RETRIEVING // RING, EARLY // RING):
                    for s in range(RING):
                        hi(r, stages["u"] + s + 2)
                        gelu(r, s)
                with act.Fori(0, GBLOCKS // 2) as pair:
                    for b in range(2):
                        for n in range(GCH):
                            r = 2 * GCH // RING * pair + (EARLY + GCH * b + n) // RING
                            s = (GCH * b + n) % RING
                            hi(r, stages["u"] + s + 2)
                            gelu(r, s)
                            act.wait_ge(gate_product, LATE * l + 2 * GCH * pair + (GCH * b + n + 3))
                            if n == 0:
                                act.wait_ge(g_stored[b], 16 * (GBLOCKS // 2) * l + 16 * pair + 16)
                            for half in range(TOK // PER_BANK):
                                t0 = n * TOK + half * PER_BANK
                                ins = act.activation(g_out[:, b, :, t0:t0 + PER_BANK],
                                                     bank[:, 2 + 2 * (s % 2) + half, :].rearrange("p (t i) -> p i t", i=P),
                                                     ACT.Copy, scale=1.0 / GATE_UP)
                            ins.then_inc(gate_copied, 1)
                        act.wait_ge(gate_copied, LATE * l + 2 * GCH * pair + (GCH * b + GCH + 2))
                        act.dma_start(g_dram[2 * pair + b], g_out[:, b, :, :]).then_inc(g_stored[b], 16)
                with act.Fori((EARLY + LATE) // RING, N_U // RING) as r:
                    for s in range(RING):
                        hi(r, stages["u"] + s + 2)
                        gelu(r, s)
                with act.Fori(0, N_V // RING - 1) as r:
                    for s in range(RING):
                        hi(r, stages["v"] + s + 2)
                for s in range(RING - 2):
                    hi(N_V // RING - 1, stages["v"] + s + 2)
            squares(2 * DEPTH, 2 * KC * DEPTH + 1)
            root(ROOTS * DEPTH)

        @block.gpsimd
        def _(pool):
            pool.memset(ones[:, :], 1.0).then_inc(consts_made, 1)
            pool.iota(iota_i, [[1, P]], base=0, channel_multiplier=0).then_inc(pool_step, 1)
            pool.wait_ge(pool_step, 1)
            pool.tensor_copy(iota_f[:, :], iota_i[:, 0:16]).then_inc(pool_step, 1)
            pool.tensor_copy(iota_b[:, :], iota_i).then_inc(consts_made, 1)
            steps = [2]
            STEPS = 18

            with pool.Fori(0, DEPTH) as l:
                pool.wait_ge(x_new, 2 * KC * l + 1)
                settle(pool)
                pool.memset(u_pad[:, :, 0:UPAD], 0.0)
                pool.memset(z_pad[:, :, 0:ZPAD], 0.0)
                pool.memset(psum_a[:, :, 0:ZPAD], 0.0).then_inc(pads_zeroed, 1)
                pool.wait_ge(pads_zeroed, l + 1)

                def lo(first, n):
                    wait_hi(pool, l, first, n)
                    pool.tensor_tensor(w_lo[:, n % 2, :], ring[:, n % RING, :], w_hi[:, n % 2, :].bitcast(F32),
                                       ALU.subtract).then_inc(tile_used[n % RING], 1)

                for n in range(N_WIN):
                    lo(0, n)

                def step(ins):
                    steps[0] += 1
                    ins.then_inc(pool_step, 1)
                    pool.wait_ge(pool_step, STEPS * l + steps[0])
                    settle(pool)

                for g, w in enumerate(WINDOWS):
                    pool.wait_ge(z_ready, CONV * l + (g + 1))
                    src, width = z_pad[:, g, :], 1
                    flip = 0
                    while width < w:
                        dst = psum_a[:, flip, :]
                        step(pool.tensor_tensor(dst[:, ZPAD:], src[:, ZPAD:], src[:, ZPAD - width:ZPAD + T - width], ALU.add))
                        src, width, flip = dst, 2 * width, 1 - flip
                    other = psum_a[:, flip, :]
                    step(pool.tensor_scalar(other[:, ZPAD:], src[:, ZPAD:], 1.0 / w, 0.0, ALU.mult, ALU.add))
                    step(pool.tensor_tensor(other[:, ZPAD:ZPAD + w], src[:, ZPAD:ZPAD + w], inv_count[:, 0:w], ALU.mult))
                    pool.tensor_tensor(pooled[:, g, :], other[:, ZPAD:], z_pad[:, g, ZPAD:], ALU.subtract)\
                        .then_inc(pooled_ready, 1)
                    pool.wait_ge(pooled_ready, CONV * l + (g + 1))
                settle(pool)
                assert steps[0] == STEPS + 2, steps

                with pool.Fori(N_WIN // RING, ROUNDS) as r:
                    for s in range(RING):
                        lo(r, s)

        @block.vector
        def _(dve):
            steps = [0]
            STEPS = 3 * 5 + 1 + CONV * TAPS + TT * (5 * (SEGS + HEADS) + 12) + 7

            dve.nop().then_inc(w_ready, RING)
            dve.wait_ge(consts_made, 2)
            dve.tensor_scalar(inv_count[:, :], iota_f[:, :], 1.0, None, ALU.add).then_inc(dve_step, 1)
            dve.wait_ge(dve_step, 1)
            dve.reciprocal(inv_count[:, :], inv_count[:, :]).then_inc(dve_step, 1)
            dve.wait_ge(dve_step, 2)
            dve.wait_ge(x_landed, 16)
            dve.nop().then_inc(x_new, 1)
            FIRST = 2
            for s in range(RING):
                dve.nop().then_inc(ada_used[s], 1)

            def modulate(s, m):
                dve.scalar_tensor_tensor(ada[:, s, :], ada[:, s, :], 1.0, cond[:, :], ALU.mult, ALU.mult,
                                         accum_out=mod_sum[:, bass.ds(m, 1)]).then_inc(ada_used[s], 1)

            dve.wait_ge(cond_ready, 1)
            with dve.Fori(0, N_ADA // RING) as r:
                for s in range(RING):
                    dve.wait_ge(ada_landed[s], 16 * r + 16)
                    modulate(s, RING * r + s)

            def count(ins):
                steps[0] += 1
                ins.then_inc(dve_step, 1)

            def rstd(l, n_root, to_var):
                v, r0, r, t = (norm_tmp[:, n, :] for n in range(4))
                to_var(v).then_inc(var_ready, 1)
                dve.wait_ge(root_ready, n_root + 1)

                def link(ins):
                    count(ins)
                    dve.wait_ge(dve_step, STEPS * l + (FIRST + steps[0]))

                link(dve.reciprocal(r, r0))
                link(dve.tensor_tensor(t, r, r, ALU.mult))
                link(dve.tensor_tensor(t, t, v, ALU.mult))
                link(dve.tensor_scalar(t, t, -0.5, 1.5, ALU.mult, ALU.add))
                link(dve.tensor_tensor(r, r, t, ALU.mult))
                return r

            def norm(l, n_norm, n_root, coefs, done):
                dve.wait_ge(summed, n_norm + 1)
                r = rstd(l, n_root, lambda v: dve.tensor_scalar(v, bank[:, 0, :], 1.0 / D, EPS, ALU.mult, ALU.add))
                for k in range(KC):
                    dve.scalar_tensor_tensor(h[:, k, :], x[:, k, :], coefs[:, k:k + 1], r, ALU.mult, ALU.mult)\
                       .then_inc(done, 1)

            with dve.Fori(0, DEPTH) as l:
                def link(ins):
                    count(ins)
                    dve.wait_ge(dve_step, STEPS * l + (FIRST + steps[0]))

                def lo_h(n_norm, n, col):
                    for k in range(KC):
                        dve.wait_ge(hi_ready_h, 3 * KC * l + (n + k + 1))
                        dve.scalar_tensor_tensor(h_lo[:, k, :], h[:, k, :], mod[:, col + k:col + k + 1],
                                                 h_hi[:, k, :].bitcast(F32), ALU.add, ALU.subtract).then_inc(lo_ready_h, 1)

                dve.wait_ge(small_landed, 16 * l + 16)
                for s in range(RING):
                    rounds_before = ADA_ROUNDS * l if s < ADA_STEP else 0 * l
                    dve.wait_ge(ada_used[s], rounds_before + (N_ADA // RING + 1))
                link(dve.tensor_tensor(mod[:, :], mod_sum[:, :], small[:, COL_BADA:COL_BADA + N_ADA], ALU.add))
                for which, (col, gain) in enumerate(((KC, COL_NORM1), (4 * KC, COL_NORM2))):
                    dve.scalar_tensor_tensor(coef[:, which, :], mod[:, col:col + KC], 1.0, small[:, gain:gain + KC],
                                             ALU.add, ALU.mult).then_inc(coef_ready, 1)
                dve.wait_ge(coef_ready, 2 * l + 2)
                norm(l, 2 * l, ROOTS * l, coef[:, 0, :], scaled)
                lo_h(2 * l, 0, 0)

                dve.wait_ge(pads_zeroed, l + 1)
                for j in range(CONV):
                    dve.wait_ge(sig_ready, CONV * l + (j + 1))
                    wait_product(dve, l, 0, 2 * j + 1)
                    dve.tensor_tensor(u_pad[:, j, UPAD:], bank[:, 2 + (2 * j + 1) % 6, :], sig[:, j % 2, :], ALU.mult)\
                       .then_inc(u_ready, 1)
                    dve.wait_ge(u_ready, CONV * l + (j + 1))
                    for k in range(TAPS):
                        w = small[:, COL_CONVW + j * TAPS + k:COL_CONVW + j * TAPS + k + 1]
                        acc = conv_y[:, j, :] if k % 2 == 0 else conv_odd
                        src = u_pad[:, j, k:k + T]
                        if k >= 2:
                            dve.wait_ge(dve_step, STEPS * l + (FIRST + steps[0] - 1))
                        if k == 0:
                            count(dve.tensor_scalar(acc, src, w, small[:, COL_CONVB + j:COL_CONVB + j + 1], ALU.mult, ALU.add))
                        elif k == 1:
                            count(dve.tensor_scalar(acc, src, w, None, ALU.mult))
                        else:
                            count(dve.scalar_tensor_tensor(acc, src, w, acc, ALU.mult, ALU.add))
                    dve.wait_ge(dve_step, STEPS * l + (FIRST + steps[0]))
                    dve.tensor_tensor(conv_y[:, j, :], conv_y[:, j, :], conv_odd, ALU.add).then_inc(conv_ready, 1)
                    dve.wait_ge(conv_ready, CONV * l + (j + 1))

                for g in range(CONV):
                    dve.wait_ge(pool_product, CONV * l + (g + 1))
                    dve.tensor_scalar(mix[:, CONV + g, :], bank[:, 4 + g, :], small[:, COL_POOLB + g:COL_POOLB + g + 1],
                                      small[:, COL_POOLS + g:COL_POOLS + g + 1], ALU.add, ALU.mult).then_inc(mix_b_ready, 1)

                dve.wait_ge(ln_summed, 2 * l + 1)
                for j in range(CONV):
                    dve.scalar_tensor_tensor(conv_y[:, j, :], bank[:, 0, :], -1.0 / (CONV * P), conv_y[:, j, :],
                                             ALU.mult, ALU.add).then_inc(centered, 1)
                dve.wait_ge(ln_summed, 2 * l + 2)
                r = rstd(l, ROOTS * l + 1,
                         lambda v: dve.tensor_scalar(v, bank[:, 0, :], 1.0 / (CONV * P), EPS, ALU.mult, ALU.add))
                for j in range(CONV):
                    dve.tensor_tensor(conv_y[:, j, :], conv_y[:, j, :], r, ALU.mult).then_inc(normed, 1)
                for n, k in enumerate([CONV + g for g in range(CONV)] + list(range(CONV))):
                    dve.wait_ge(hi_ready_h, 3 * KC * l + (KC + n + 1))
                    dve.tensor_tensor(h_lo[:, k, :], mix[:, k, :], h_hi[:, k, :].bitcast(F32), ALU.subtract)\
                       .then_inc(lo_ready_h, 1)

                for n in range(N_WOUT):
                    wait_product(dve, l, 0, stages["wout"] + n)
                    dve.scalar_tensor_tensor(x[:, n, :], bank[:, 2 + n % 6, :], mod[:, 2 * KC + n:2 * KC + n + 1],
                                             x[:, n, :], ALU.mult, ALU.add).then_inc(x_new, 1)
                norm(l, 2 * l + 1, ROOTS * l + 2, coef[:, 1, :], scaled)
                lo_h(2 * l + 1, 2 * KC, 3 * KC)

                dve.wait_ge(q_ready, N_WQ * l + N_WQ)
                dve.wait_ge(lo_ready_h, 3 * KC * l + 3 * KC)

                def every(n, make):
                    for s in range(n):
                        count(make(s))
                    dve.wait_ge(dve_step, STEPS * l + (FIRST + steps[0]))
                    settle(dve)

                def top16(n, values, spare, v_of, i_of):
                    every(n, lambda s: dve.max(v_of(s)[:, 0:8], values(s)))
                    every(n, lambda s: dve.max_index(i_of(s)[:, 0:8], v_of(s)[:, 0:8], values(s)))
                    every(n, lambda s: dve.match_replace(spare(s), v_of(s)[:, 0:8], values(s), LOWEST))
                    every(n, lambda s: dve.max(v_of(s)[:, 8:16], spare(s)))
                    every(n, lambda s: dve.max_index(i_of(s)[:, 8:16], v_of(s)[:, 8:16], spare(s)))

                big_s = big.rearrange("p (s k) -> p s k", k=P)
                big_c = big.rearrange("p (s k) -> p s k", k=TOPK * TOPK)
                big_4 = big.rearrange("p (s i j) -> p s i j", i=TOPK, j=TOPK)
                eq_4 = big2.rearrange("p (s i j) -> p s i j", i=TOPK, j=TOPK)
                shape4 = [P, HEADS, TOPK, TOPK]
                v2 = vals.rearrange("p (h e) k -> p h e k", e=2)
                i2 = idx_f.rearrange("p (h e) k -> p h e k", e=2)
                bj_v = bj.rearrange("p (s k) -> p s k", k=TOPK)
                for a in range(TT):
                    dve.wait_ge(score_ready, 4 * TT * l + 4 * (a + 1))
                    settle(dve)
                    sc_a = scores[:, a, :, :]
                    sc_c = sc_a.rearrange("p s k -> p (s k)").rearrange("p (s k) -> p s k", k=TOPK * TOPK)
                    top16(SEGS, lambda s: sc_a[:, s, :], lambda s: big_s[:, s, :], lambda s: vals[:, s, :],
                          lambda s: idx_u[:, s, :])
                    link(dve.tensor_tensor(big_4, v2[:, :, 0, :].unsqueeze(3).to_broadcast(shape4),
                                           v2[:, :, 1, :].unsqueeze(2).to_broadcast(shape4), ALU.add))
                    settle(dve)
                    top16(HEADS, lambda s: big_c[:, s, :], lambda s: sc_c[:, s, :], lambda s: best[:, s, :],
                          lambda s: bj_v[:, s, :])
                    count(dve.tensor_scalar(ja_u, bj, 4, None, ALU.logical_shift_right))
                    link(dve.tensor_scalar(jb_u, bj, TOPK - 1, None, ALU.bitwise_and))
                    count(dve.tensor_copy(idx_f[:, :, :], idx_u[:, :, :]))
                    count(dve.tensor_copy(ja_f.rearrange("p s k -> p (s k)"), ja_u))
                    link(dve.tensor_copy(jb_f.rearrange("p s k -> p (s k)"), jb_u))
                    for half, (jf, to) in enumerate(((ja_f, i1_f), (jb_f, i2_f))):
                        link(dve.tensor_tensor(eq_4, jf.unsqueeze(3).to_broadcast(shape4),
                                               iota_f[:, :].unsqueeze(1).unsqueeze(1).to_broadcast(shape4), ALU.is_equal))
                        link(dve.tensor_tensor(eq_4, eq_4, i2[:, :, half, :].unsqueeze(2).to_broadcast(shape4), ALU.mult))
                        link(dve.tensor_reduce(to[:, a, :].rearrange("p (h k) -> p h k", k=TOPK), eq_4, AX_X, ALU.add))
                    dve.tensor_tensor(gate[:, a, :].rearrange("p (h k) -> p h k", k=TOPK), best[:, :, :],
                                      best[:, :, 0:1].to_broadcast([P, HEADS, TOPK]), ALU.subtract).then_inc(retrieved, 1)
                    dve.wait_ge(retrieved, TT * l + (a + 1))
                dve.wait_ge(exp_done, l + 1)
                gate_v = gate.rearrange("p a (h k) -> p (a h) k", k=TOPK)
                link(dve.tensor_reduce(gsum, gate_v, AX_X, ALU.add))
                link(dve.reciprocal(ginv, gsum))
                dve.tensor_tensor(gate_v, gate_v, ginv.unsqueeze(2).to_broadcast([P, TT * HEADS, TOPK]), ALU.mult)\
                   .then_inc(gate_ready, 1)
                dve.wait_ge(turned, l + 1)
                count(dve.tensor_copy(i1_t, bank[:, 2, :]))
                count(dve.tensor_copy(i2_t, bank[:, 3, :]))
                gb = hf[:, 3 * T:4 * T].bitcast(F16)[:, 0:T]
                link(dve.tensor_scalar(gb, bank[:, 4, :], GATE_UP, None, ALU.mult))
                link(dve.tensor_copy(ghi_t, gb))
                link(dve.scalar_tensor_tensor(glo_t, bank[:, 4, :], GATE_UP, ghi_t, ALU.mult, ALU.subtract))
                settle(dve)

                with dve.Fori(0, LATE // RING) as r:
                    for s in range(RING):
                        b = s % 2
                        dve.wait_ge(gate_product, LATE * l + RING * r + (s + 1))
                        for j in range(TOK):
                            t = RING * TOK * r + (s * TOK + j)
                            col = bass.ds(t, 1)
                            dve.tensor_scalar(hot2[:, b, j, :], iota_b[:, :], i2_t[:, col], None, ALU.is_equal)
                            for q, g_part in enumerate((ghi_t, glo_t)):
                                ins = dve.tensor_scalar(hot1[:, b, j, q, :], iota_b[:, :], i1_t[:, col], g_part[:, col],
                                                        ALU.is_equal, ALU.mult)
                        ins.then_inc(hot_ready, 1)

                def weights(r, s):
                    b = s % 2
                    dve.wait_ge(ga_landed[s], 16 * (N_V // RING) * l + 16 * r + 16)
                    dve.wait_ge(g_landed[s], 16 * (N_V // RING) * l + 16 * r + 16)
                    dve.tensor_tensor(ga_in[:, s, :], ga_in[:, s, :], g_in[:, s, :], ALU.mult).then_inc(w_step, 1)
                    dve.wait_ge(w_step, 2 * N_V * l + 2 * RING * r + (2 * s + 1))
                    wait_product(dve, l, r, stages["v"] + s - 2)
                    dve.tensor_copy(v_hi[:, b, :], ga_in[:, s, :]).then_inc(w_step, 1)
                    dve.wait_ge(w_step, 2 * N_V * l + 2 * RING * r + (2 * s + 2))
                    dve.tensor_tensor(v_lo[:, b, :], ga_in[:, s, :], v_hi[:, b, :].bitcast(F32), ALU.subtract)\
                       .then_inc(w_ready, 1)

                def rounds(start, end, with_ada):
                    with dve.Fori(start, end) as r:
                        for s in range(RING):
                            weights(r, s)
                            if with_ada and s < ADA_STEP:
                                wait_ada(dve, ada_landed, 16, l, s, r)
                                modulate(s, ADA_STEP * r + s)

                with dve.If(l < LAST):
                    rounds(0, ADA_ROUNDS, True)
                with dve.Else():
                    rounds(0, ADA_ROUNDS, False)
                rounds(ADA_ROUNDS, N_V // RING, False)
                dve.wait_ge(chunk_done, CHUNKS * l + CHUNKS + 2)
                for k in range(KC):
                    dve.scalar_tensor_tensor(x[:, k, :], bank[:, k, :], mod[:, 5 * KC + k:5 * KC + k + 1],
                                             x[:, k, :], ALU.mult, ALU.add).then_inc(x_new, 1)
                assert steps[0] == STEPS, steps
            steps[0] = 0
            norm(DEPTH, 2 * DEPTH, ROOTS * DEPTH, finalg, out_ready)


def kernel(**inputs):
    import numpy as np
    import concourse.bacc as bacc
    from concourse.bass_utils import run_bass_kernel_spmd

    L = inputs["w_ada"].shape[0]
    D = inputs["w_ada"].shape[1]
    KC = D // P

    def tiles(w):
        n = w.shape[2] // P
        return np.ascontiguousarray(w.reshape(L, KC, P, n, P).transpose(0, 3, 2, 1, 4).reshape(L, n, P, KC * P))

    def columns(v):
        return v.reshape(L, -1, P).transpose(0, 2, 1)

    a = {k: np.asarray(v) for k, v in inputs.items()}
    conv = a["conv_w"].shape[2] // P
    order = [b for j in range(conv) for b in (conv + j, j)] + list(range(2 * conv, 3 * conv))
    experts = a["peer_u"].shape[1] // P
    taps = a["conv_w"].transpose(0, 2, 1).reshape(L, conv, P, -1).transpose(0, 2, 1, 3).reshape(L, P, -1)
    arrays = {
        "x_in": a["x"][0].T.reshape(KC, P, -1).transpose(1, 0, 2),
        "c_in": a["c"],
        "ada_t": a["w_ada"].transpose(0, 2, 1).reshape(L, -1, P, D),
        "win_t": tiles(a["w_in"])[:, order],
        "wout_t": tiles(a["w_out"]),
        "wq_t": tiles(a["peer_wq"]),
        "u_t": a["peer_u"].reshape(L, experts, P, KC, P).transpose(0, 1, 4, 3, 2).reshape(L, experts, P, D),
        "v_t": a["peer_v"].reshape(L, experts, P, D),
        "keys_in": a["peer_keys"].transpose(0, 4, 1, 2, 3).reshape(L, P, -1, P),
        "poolw_in": a["pool_w"].transpose(0, 2, 1, 3),
        "small_in": np.concatenate([
            columns(a["norm1_g"]), columns(a["norm2_g"]), columns(a["b_ada"]), columns(a["conv_b"]),
            columns(a["conv_ln_g"]), columns(a["conv_ln_b"]), columns(a["pool_b"].reshape(L, -1)),
            columns(a["pool_scale"]), taps], axis=2),
        "finalg_in": a["final_g"].reshape(KC, P).T,
        "ident_in": np.eye(P, dtype=np.float32),
    }
    nc = bacc.Bacc("TRN2", target_bir_lowering=False, num_devices=1)
    args = {}
    for name, v in arrays.items():
        arrays[name] = v = np.ascontiguousarray(v)
        args[name] = nc.dram_tensor(name, v.shape, mybir.dt.from_np(v.dtype), kind="ExternalInput").ap()
    seq = a["x"].shape[1]
    out = nc.dram_tensor("out", [P, KC, seq], F32, kind="ExternalOutput").ap()
    hybrid_encoder(nc, out=out, **args)
    got = run_bass_kernel_spmd(nc, [arrays], core_ids=[0]).results[0]["out"]
    return np.ascontiguousarray(got.transpose(2, 1, 0).reshape(1, seq, D))
```
